# Optimizing a Trainium2 kernel written in Bass

```python
import math
import jax, jax.numpy as jnp
from jax import lax
import numpy as np

D_MODEL = 1024
BATCH = 1
SEQ = 256
DEPTH = 1

FOX_HEADS = 8
FOX_HEAD_DIM = 128
FOX_WIDTH = FOX_HEADS * FOX_HEAD_DIM
FOX_BLOCK = 128
GDN_HEADS = 8
GDN_HEAD_K = 128
GDN_HEAD_V = 128
GDN_K_WIDTH = GDN_HEADS * GDN_HEAD_K
GDN_V_WIDTH = GDN_HEADS * GDN_HEAD_V
GDN_CONV = 4
GDN_CONV_CH = 2 * GDN_K_WIDTH + GDN_V_WIDTH
GDN_CHUNK = 64
D_FF = 2816
FFN_CONV = 3
EPS = 1e-6

IN_SIZES = (FOX_WIDTH, FOX_WIDTH, FOX_WIDTH, FOX_HEADS,
            GDN_K_WIDTH, GDN_K_WIDTH, GDN_V_WIDTH, GDN_HEADS, GDN_HEADS, GDN_V_WIDTH,
            D_MODEL, D_MODEL)
D_IN = sum(IN_SIZES)


def rmsnorm(x, g):
    xf = x.astype(jnp.float32)
    xf = xf * lax.rsqrt(jnp.mean(xf * xf, axis=-1, keepdims=True) + EPS)
    return (xf * g.astype(jnp.float32)).astype(x.dtype)

def l2norm(x):
    xf = x.astype(jnp.float32)
    return xf * lax.rsqrt(jnp.sum(xf * xf, axis=-1, keepdims=True) + EPS)

def causal_dwconv(x, w):
    K = w.shape[0]
    S = x.shape[1]
    xp = jnp.pad(x, ((0, 0), (K - 1, 0), (0, 0)))
    return sum(xp[:, i:i + S, :] * w[i] for i in range(K))

def split_in(h):
    idx = np.cumsum(np.array(IN_SIZES))[:-1].tolist()
    return jnp.split(h, idx, axis=-1)

def fox_attention(q, k, v, log_f):
    B, S, H, Dh = q.shape
    nb = S // FOX_BLOCK
    scale = Dh ** -0.5
    c = jnp.cumsum(log_f.astype(jnp.float32), axis=1).transpose(0, 2, 1)
    kh = k.transpose(0, 2, 1, 3)
    vh = v.transpose(0, 2, 1, 3)
    qb = q.reshape(B, nb, FOX_BLOCK, H, Dh).transpose(1, 0, 3, 2, 4)
    cb = c.reshape(B, H, nb, FOX_BLOCK).transpose(2, 0, 1, 3)
    key_pos = jnp.arange(S)

    def block(args):
        qi, ci, i = args
        s = jnp.einsum('bhqd,bhkd->bhqk', qi, kh).astype(jnp.float32) * scale
        s = s + (ci[..., :, None] - c[..., None, :])
        q_pos = i * FOX_BLOCK + jnp.arange(FOX_BLOCK)
        causal = key_pos[None, :] <= q_pos[:, None]
        p = jax.nn.softmax(jnp.where(causal, s, -jnp.inf), axis=-1)
        return jnp.einsum('bhqk,bhkd->bhqd', p.astype(vh.dtype), vh)

    o = lax.map(block, (qb, cb, jnp.arange(nb)))
    return o.transpose(1, 0, 3, 2, 4).reshape(B, S, H * Dh)

def gated_delta_rule(q, k, v, g, beta):
    B, S, H, dk = q.shape
    dv = v.shape[-1]
    C = GDN_CHUNK
    N = S // C
    f32 = jnp.float32

    def chunk4(t):
        return t.astype(f32).reshape(B, N, C, H, t.shape[-1]).transpose(0, 3, 1, 2, 4)

    def chunk3(t):
        return t.astype(f32).reshape(B, N, C, H).transpose(0, 3, 1, 2)

    qc = chunk4(q) * (dk ** -0.5)
    kc = chunk4(k)
    vc = chunk4(v)
    bc = chunk3(beta)
    gc = jnp.cumsum(chunk3(g), axis=-1)

    tri_incl = jnp.tril(jnp.ones((C, C), dtype=bool))
    tri_strict = jnp.tril(jnp.ones((C, C), dtype=bool), k=-1)
    diff = gc[..., :, None] - gc[..., None, :]
    decay = jnp.exp(jnp.where(tri_incl, diff, -jnp.inf))

    kb = kc * bc[..., None]
    A = jnp.where(tri_strict, jnp.einsum('bhncd,bhnmd->bhncm', kb, kc) * decay, 0.0)
    lhs = A + jnp.eye(C, dtype=f32)
    rhs = jnp.concatenate([vc * bc[..., None], kb * jnp.exp(gc)[..., None]], axis=-1)
    sol = lax.linalg.triangular_solve(lhs, rhs, left_side=True, lower=True, unit_diagonal=True)
    u_hat, w = sol[..., :dv], sol[..., dv:]

    attn = jnp.einsum('bhncd,bhnmd->bhncm', qc, kc) * decay
    q_dec = qc * jnp.exp(gc)[..., None]
    k_dec = kc * jnp.exp(gc[..., -1:] - gc)[..., None]
    g_last = jnp.exp(gc[..., -1])

    xs = tuple(jnp.moveaxis(t, 2, 0) for t in (u_hat, w, attn, q_dec, k_dec, g_last))

    def step(state, inp):
        u_hat_i, w_i, attn_i, q_dec_i, k_dec_i, gl_i = inp
        u = u_hat_i - jnp.einsum('bhcd,bhdv->bhcv', w_i, state)
        o = jnp.einsum('bhcd,bhdv->bhcv', q_dec_i, state) + jnp.einsum('bhcm,bhmv->bhcv', attn_i, u)
        state = state * gl_i[..., None, None] + jnp.einsum('bhcd,bhcv->bhdv', k_dec_i, u)
        return state, o

    s0 = jnp.zeros((B, H, dk, dv), f32)
    _, o = lax.scan(step, s0, xs)
    return o.transpose(1, 0, 3, 2, 4).reshape(B, S, H, dv).astype(v.dtype)

def first_inputs(seed: int = 0) -> dict:
    key = jax.random.key(seed)
    ks = jax.random.split(key, 20)
    L, D = DEPTH, D_MODEL
    nrm = jax.random.normal
    x = nrm(ks[0], (BATCH, SEQ, D), jnp.float32)
    norm_mix = 1.0 + 0.05 * nrm(ks[1], (L, D), jnp.float32)
    w_in = nrm(ks[2], (L, D, D_IN), jnp.float32) * D ** -0.5
    fox_f_bias = 3.0 + 0.5 * nrm(ks[3], (L, FOX_HEADS), jnp.float32)
    gdn_conv_w = nrm(ks[4], (L, GDN_CONV, GDN_CONV_CH), jnp.float32) * GDN_CONV ** -0.5
    gdn_a_log = jnp.log(jax.random.uniform(ks[5], (L, GDN_HEADS), jnp.float32, 1.0, 16.0))
    dt = jnp.exp(jax.random.uniform(ks[6], (L, GDN_HEADS), jnp.float32, math.log(1e-3), math.log(1e-1)))
    gdn_dt_bias = dt + jnp.log(-jnp.expm1(-dt))
    gdn_norm = 1.0 + 0.05 * nrm(ks[7], (L, GDN_HEAD_V), jnp.float32)
    w_branch_fox = nrm(ks[8], (L, FOX_WIDTH, D), jnp.float32) * FOX_WIDTH ** -0.5
    w_branch_gdn = nrm(ks[9], (L, GDN_V_WIDTH, D), jnp.float32) * GDN_V_WIDTH ** -0.5
    w_out = nrm(ks[10], (L, D, D), jnp.float32) * D ** -0.5
    norm_ffn = 1.0 + 0.05 * nrm(ks[11], (L, D), jnp.float32)
    w_up = nrm(ks[12], (L, D, 2 * D_FF), jnp.float32) * D ** -0.5
    ffn_conv_w = nrm(ks[13], (L, FFN_CONV, 2 * D_FF), jnp.float32) * FFN_CONV ** -0.5
    w_down = nrm(ks[14], (L, D_FF, D), jnp.float32) * D_FF ** -0.5
    norm_final = 1.0 + 0.05 * nrm(ks[15], (D,), jnp.float32)
    return {"x": x, "norm_mix": norm_mix, "w_in": w_in, "fox_f_bias": fox_f_bias,
            "gdn_conv_w": gdn_conv_w, "gdn_a_log": gdn_a_log, "gdn_dt_bias": gdn_dt_bias,
            "gdn_norm": gdn_norm, "w_branch_fox": w_branch_fox, "w_branch_gdn": w_branch_gdn,
            "w_out": w_out, "norm_ffn": norm_ffn, "w_up": w_up, "ffn_conv_w": ffn_conv_w,
            "w_down": w_down, "norm_final": norm_final}

def first_block(x, norm_mix, w_in, fox_f_bias, gdn_conv_w, gdn_a_log, gdn_dt_bias, gdn_norm,
              w_branch_fox, w_branch_gdn, w_out, norm_ffn, w_up, ffn_conv_w, w_down, norm_final):
    B, S, D = x.shape
    h = x
    for l in range(DEPTH):
        hn = rmsnorm(h, norm_mix[l])
        proj = jnp.einsum('bsd,de->bse', hn, w_in[l])
        (fq, fk, fv, ff, gq, gk, gv, ga, gb, gz, gate_fox, gate_gdn) = split_in(proj)

        log_f = jax.nn.log_sigmoid(ff.astype(jnp.float32) + fox_f_bias[l].astype(jnp.float32))
        y_fox = fox_attention(fq.reshape(B, S, FOX_HEADS, FOX_HEAD_DIM),
                              fk.reshape(B, S, FOX_HEADS, FOX_HEAD_DIM),
                              fv.reshape(B, S, FOX_HEADS, FOX_HEAD_DIM), log_f)

        qkv = jax.nn.silu(causal_dwconv(jnp.concatenate([gq, gk, gv], axis=-1), gdn_conv_w[l]))
        cq, ck, cv = jnp.split(qkv, [GDN_K_WIDTH, 2 * GDN_K_WIDTH], axis=-1)
        q = l2norm(cq.reshape(B, S, GDN_HEADS, GDN_HEAD_K))
        k = l2norm(ck.reshape(B, S, GDN_HEADS, GDN_HEAD_K))
        v = cv.reshape(B, S, GDN_HEADS, GDN_HEAD_V)
        g = -jnp.exp(gdn_a_log[l].astype(jnp.float32)) * jax.nn.softplus(
            ga.astype(jnp.float32) + gdn_dt_bias[l].astype(jnp.float32))
        beta = jax.nn.sigmoid(gb.astype(jnp.float32))
        o = gated_delta_rule(q, k, v, g, beta)
        o = rmsnorm(o, gdn_norm[l]) * jax.nn.silu(gz.reshape(B, S, GDN_HEADS, GDN_HEAD_V))
        y_gdn = o.reshape(B, S, GDN_V_WIDTH)

        y = (jax.nn.sigmoid(gate_fox) * jnp.einsum('bse,ed->bsd', y_fox, w_branch_fox[l])
             + jax.nn.sigmoid(gate_gdn) * jnp.einsum('bse,ed->bsd', y_gdn, w_branch_gdn[l]))
        h = h + jnp.einsum('bsd,de->bse', y, w_out[l])

        hn = rmsnorm(h, norm_ffn[l])
        up = causal_dwconv(jnp.einsum('bsd,df->bsf', hn, w_up[l]), ffn_conv_w[l])
        u_gate, u_val = jnp.split(up, 2, axis=-1)
        h = h + jnp.einsum('bsf,fd->bsd', jax.nn.silu(u_gate) * u_val, w_down[l])
    return rmsnorm(h, norm_final)


DEPTH_2 = 4

N_MIXERS = 3
D_FF_2 = 4 * D_MODEL
RMS_EPS = 1e-6
Q_BLOCK = 128

N_BUCKETS = 32
MAX_DISTANCE = 128
N_BIAS_HEADS = 16

A_HEADS = 16
A_HEAD_DIM = 64
IDX_HEADS = 8
IDX_DIM = 64
TOPK_MAX = 256
A_IN = A_HEADS * A_HEAD_DIM + 2 * A_HEAD_DIM + IDX_HEADS * IDX_DIM + IDX_DIM + IDX_HEADS

B_HEADS = 16
B_KV_HEADS = 4
B_HEAD_DIM = 64
WINDOW = 128
B_IN = (B_HEADS + 2 * B_KV_HEADS) * B_HEAD_DIM

C_HEADS = 16
C_Q_RANK = 256
C_KV_RANK = 128
C_NOPE = 64
C_ROPE = 32
C_V = 64
C_QK = C_NOPE + C_ROPE
C_IN = C_Q_RANK + C_KV_RANK + C_ROPE
ROPE_THETA = 10000.0

N_A = (DEPTH_2 + 2) // 3
N_B = (DEPTH_2 + 1) // 3
N_C = DEPTH_2 // 3


def rms_norm(x, g):
    xf = x.astype(jnp.float32)
    y = xf * lax.rsqrt(jnp.mean(xf * xf, axis=-1, keepdims=True) + RMS_EPS)
    return (y * g.astype(jnp.float32)).astype(x.dtype)

def split_cols(t, sizes):
    return jnp.split(t, np.cumsum(sizes)[:-1].tolist(), axis=-1)

def t5_bucket(rel):
    n = jnp.maximum(rel, 0)
    max_exact = N_BUCKETS // 2
    nf = jnp.maximum(n, 1).astype(jnp.float32)
    large = max_exact + (jnp.log(nf / max_exact) / math.log(MAX_DISTANCE / max_exact)
                         * (N_BUCKETS - max_exact)).astype(jnp.int32)
    large = jnp.minimum(large, N_BUCKETS - 1)
    return jnp.where(n < max_exact, n, large)

def to_blocks(t, nb):
    return jnp.moveaxis(t.reshape(t.shape[0], nb, Q_BLOCK, *t.shape[2:]), 1, 0)

def from_blocks(t):
    t = jnp.moveaxis(t, 0, 1)
    return t.reshape(t.shape[0], t.shape[1] * t.shape[2], *t.shape[3:])

def dsa_mixer(h, w_in, q_gain, k_gain, w_out, rel_bias):
    B, L, _ = h.shape
    nb = L // Q_BLOCK
    k_sel = min(TOPK_MAX, L // 4)
    q, k, v, q_idx, k_idx, w_idx = split_cols(
        h @ w_in, [A_HEADS * A_HEAD_DIM, A_HEAD_DIM, A_HEAD_DIM, IDX_HEADS * IDX_DIM, IDX_DIM, IDX_HEADS])
    q = rms_norm(q.reshape(B, L, A_HEADS, A_HEAD_DIM), q_gain)
    k = rms_norm(k, k_gain)
    q_idx = q_idx.reshape(B, L, IDX_HEADS, IDX_DIM)
    w_idx = w_idx * IDX_HEADS ** -0.5
    key_pos = jnp.arange(L, dtype=jnp.int32)
    q_pos = key_pos.reshape(nb, Q_BLOCK)
    scale = A_HEAD_DIM ** -0.5

    def block(args):
        qb, qib, wb, pos = args
        s_idx = jnp.einsum('bqhd,bsd->bqhs', qib, k_idx) * IDX_DIM ** -0.5
        score = jnp.einsum('bqh,bqhs->bqs', wb, jax.nn.relu(s_idx)).astype(jnp.float32)
        admissible = key_pos[None, :] <= pos[:, None]
        score = jnp.where(admissible[None], score, -jnp.inf)
        _, sel = lax.top_k(score, k_sel)
        kg = jax.vmap(lambda kk, ii: kk[ii])(k, sel)
        vg = jax.vmap(lambda vv, ii: vv[ii])(v, sel)
        rel = pos[None, :, None] - sel
        bias = jnp.moveaxis(rel_bias[t5_bucket(rel)], -1, 1)
        logits = jnp.einsum('bqhd,bqjd->bhqj', qb, kg).astype(jnp.float32) * scale + bias
        logits = jnp.where((rel >= 0)[:, None], logits, -jnp.inf)
        p = jax.nn.softmax(logits, axis=-1).astype(vg.dtype)
        return jnp.einsum('bhqj,bqjd->bqhd', p, vg)

    out = lax.map(block, (to_blocks(q, nb), to_blocks(q_idx, nb), to_blocks(w_idx, nb), q_pos))
    return from_blocks(out).reshape(B, L, A_HEADS * A_HEAD_DIM) @ w_out

def swa_mixer(h, w_in, q_gain, k_gain, sinks, w_out, rel_bias):
    B, L, _ = h.shape
    nb = L // WINDOW
    group = B_HEADS // B_KV_HEADS
    q, k, v = split_cols(h @ w_in, [B_HEADS * B_HEAD_DIM, B_KV_HEADS * B_HEAD_DIM, B_KV_HEADS * B_HEAD_DIM])
    q = rms_norm(q.reshape(B, L, B_HEADS, B_HEAD_DIM), q_gain).reshape(B, L, B_KV_HEADS, group, B_HEAD_DIM)
    k = rms_norm(k.reshape(B, L, B_KV_HEADS, B_HEAD_DIM), k_gain)
    v = v.reshape(B, L, B_KV_HEADS, B_HEAD_DIM)

    def band(t):
        tb = t.reshape(B, nb, WINDOW, B_KV_HEADS, B_HEAD_DIM)
        prev = jnp.pad(tb[:, :-1], ((0, 0), (1, 0), (0, 0), (0, 0), (0, 0)))
        return jnp.moveaxis(jnp.concatenate([prev, tb], axis=2), 1, 0)

    kb, vb = band(k), band(v)
    qi = jnp.arange(WINDOW, dtype=jnp.int32)[:, None] + WINDOW
    kj = jnp.arange(2 * WINDOW, dtype=jnp.int32)[None, :]
    rel = qi - kj
    in_band = (rel >= 0) & (rel < WINDOW)
    bias = jnp.transpose(rel_bias[t5_bucket(rel)], (2, 0, 1)).reshape(B_KV_HEADS, group, WINDOW, 2 * WINDOW)
    sink = sinks.astype(jnp.float32).reshape(B_KV_HEADS, group, 1, 1)
    scale = B_HEAD_DIM ** -0.5

    def block(args):
        qb, kbb, vbb, n = args
        logits = jnp.einsum('bqkgd,bjkd->bkgqj', qb, kbb).astype(jnp.float32) * scale + bias
        ok = in_band & ((n > 0) | (kj >= WINDOW))
        logits = jnp.where(ok, logits, -jnp.inf)
        m = jnp.maximum(jnp.max(logits, axis=-1, keepdims=True), sink)
        e = jnp.exp(logits - m)
        p = e / (jnp.sum(e, axis=-1, keepdims=True) + jnp.exp(sink - m))
        return jnp.einsum('bkgqj,bjkd->bqkgd', p.astype(vbb.dtype), vbb)

    out = lax.map(block, (to_blocks(q, nb), kb, vb, jnp.arange(nb, dtype=jnp.int32)))
    return from_blocks(out).reshape(B, L, B_HEADS * B_HEAD_DIM) @ w_out

def apply_rope(t, cos, sin):
    t1, t2 = jnp.split(t, 2, axis=-1)
    return jnp.concatenate([t1 * cos - t2 * sin, t2 * cos + t1 * sin], axis=-1).astype(t.dtype)

def mla_mixer(h, positions, w_in, q_a_gain, w_q_b, kv_a_gain, w_kv_b, q_gain, k_gain, w_out):
    B, L, _ = h.shape
    nb = L // Q_BLOCK
    q_lat, kv_lat, k_rope = split_cols(h @ w_in, [C_Q_RANK, C_KV_RANK, C_ROPE])
    q = (rms_norm(q_lat, q_a_gain) @ w_q_b).reshape(B, L, C_HEADS, C_QK)
    kv = (rms_norm(kv_lat, kv_a_gain) @ w_kv_b).reshape(B, L, C_HEADS, C_NOPE + C_V)
    k_nope, v = split_cols(kv, [C_NOPE, C_V])
    k = jnp.concatenate([k_nope, jnp.broadcast_to(k_rope[:, :, None, :], (B, L, C_HEADS, C_ROPE))], axis=-1)
    q = rms_norm(q, q_gain)
    k = rms_norm(k, k_gain)
    inv_freq = ROPE_THETA ** (-jnp.arange(0, C_ROPE, 2, dtype=jnp.float32) / C_ROPE)
    ang = positions.astype(jnp.float32)[..., None] * inv_freq
    cos, sin = jnp.cos(ang)[:, :, None, :], jnp.sin(ang)[:, :, None, :]
    q = jnp.concatenate([q[..., :C_NOPE], apply_rope(q[..., C_NOPE:], cos, sin)], axis=-1)
    k = jnp.concatenate([k[..., :C_NOPE], apply_rope(k[..., C_NOPE:], cos, sin)], axis=-1)
    key_pos = jnp.arange(L, dtype=jnp.int32)
    scale = C_QK ** -0.5

    def block(args):
        qb, pos = args
        logits = jnp.einsum('bqhd,bshd->bhqs', qb, k).astype(jnp.float32) * scale
        logits = jnp.where(key_pos[None, :] <= pos[:, None], logits, -jnp.inf)
        p = jax.nn.softmax(logits, axis=-1).astype(v.dtype)
        return jnp.einsum('bhqs,bshd->bqhd', p, v)

    out = lax.map(block, (to_blocks(q, nb), key_pos.reshape(nb, Q_BLOCK)))
    return from_blocks(out).reshape(B, L, C_HEADS * C_V) @ w_out

def sqrelu_mlp(h, w_up, w_down):
    return jnp.square(jax.nn.relu(h @ w_up)) @ w_down

def second_inputs(seed: int = 0) -> dict:
    key = jax.random.key(seed)
    ks = jax.random.split(key, 24)
    f32 = jnp.float32

    def w(k, shape, fan_in):
        return jax.random.normal(k, shape, f32) * fan_in ** -0.5

    def gain(k, shape):
        return 1.0 + 0.02 * jax.random.normal(k, shape, f32)

    x = jax.random.normal(ks[0], (BATCH, SEQ, D_MODEL), f32)
    start = jax.random.randint(ks[1], (BATCH, 1), 0, 1024, dtype=jnp.int32)
    positions = start + jnp.arange(SEQ, dtype=jnp.int32)[None, :]
    return {
        'x': x,
        'positions': positions,
        'rel_bias': 0.5 * jax.random.normal(ks[2], (N_BUCKETS, N_BIAS_HEADS), f32),
        'norm_mix': gain(ks[3], (DEPTH_2, D_MODEL)),
        'norm_mlp': gain(ks[4], (DEPTH_2, D_MODEL)),
        'w_up': w(ks[5], (DEPTH_2, D_MODEL, D_FF_2), D_MODEL),
        'w_down': w(ks[6], (DEPTH_2, D_FF_2, D_MODEL), D_FF_2),
        'a_w_in': w(ks[7], (N_A, D_MODEL, A_IN), D_MODEL),
        'a_q_gain': gain(ks[8], (N_A, A_HEAD_DIM)),
        'a_k_gain': gain(ks[9], (N_A, A_HEAD_DIM)),
        'a_w_out': w(ks[10], (N_A, A_HEADS * A_HEAD_DIM, D_MODEL), A_HEADS * A_HEAD_DIM),
        'b_w_in': w(ks[11], (N_B, D_MODEL, B_IN), D_MODEL),
        'b_q_gain': gain(ks[12], (N_B, B_HEAD_DIM)),
        'b_k_gain': gain(ks[13], (N_B, B_HEAD_DIM)),
        'b_sinks': jax.random.normal(ks[14], (N_B, B_HEADS), f32),
        'b_w_out': w(ks[15], (N_B, B_HEADS * B_HEAD_DIM, D_MODEL), B_HEADS * B_HEAD_DIM),
        'c_w_in': w(ks[16], (N_C, D_MODEL, C_IN), D_MODEL),
        'c_q_a_gain': gain(ks[17], (N_C, C_Q_RANK)),
        'c_w_q_b': w(ks[18], (N_C, C_Q_RANK, C_HEADS * C_QK), C_Q_RANK),
        'c_kv_a_gain': gain(ks[19], (N_C, C_KV_RANK)),
        'c_w_kv_b': w(ks[20], (N_C, C_KV_RANK, C_HEADS * (C_NOPE + C_V)), C_KV_RANK),
        'c_q_gain': gain(ks[21], (N_C, C_QK)),
        'c_k_gain': gain(ks[22], (N_C, C_QK)),
        'c_w_out': w(ks[23], (N_C, C_HEADS * C_V, D_MODEL), C_HEADS * C_V),
    }

def second_block(x, positions, rel_bias, norm_mix, norm_mlp, w_up, w_down,
              a_w_in, a_q_gain, a_k_gain, a_w_out,
              b_w_in, b_q_gain, b_k_gain, b_sinks, b_w_out,
              c_w_in, c_q_a_gain, c_w_q_b, c_kv_a_gain, c_w_kv_b, c_q_gain, c_k_gain, c_w_out):
    ia = ib = ic = 0
    for i in range(DEPTH_2):
        h = rms_norm(x, norm_mix[i])
        kind = i % N_MIXERS
        if kind == 0:
            y = dsa_mixer(h, a_w_in[ia], a_q_gain[ia], a_k_gain[ia], a_w_out[ia], rel_bias)
            ia += 1
        elif kind == 1:
            y = swa_mixer(h, b_w_in[ib], b_q_gain[ib], b_k_gain[ib], b_sinks[ib], b_w_out[ib], rel_bias)
            ib += 1
        else:
            y = mla_mixer(h, positions, c_w_in[ic], c_q_a_gain[ic], c_w_q_b[ic], c_kv_a_gain[ic],
                          c_w_kv_b[ic], c_q_gain[ic], c_k_gain[ic], c_w_out[ic])
            ic += 1
        x = x + y
        x = x + sqrelu_mlp(rms_norm(x, norm_mlp[i]), w_up[i], w_down[i])
    return x


def setup_inputs(seed=0):
    out = dict(first_inputs(seed))
    for name, value in second_inputs(seed + 1).items():
        if name != "x":
            out[name + "_2"] = value
    return out


def reference(
    x, norm_mix, w_in, fox_f_bias, gdn_conv_w, gdn_a_log, gdn_dt_bias, gdn_norm, w_branch_fox,
    w_branch_gdn, w_out, norm_ffn, w_up, ffn_conv_w, w_down, norm_final, positions_2,
    rel_bias_2, norm_mix_2, norm_mlp_2, w_up_2, w_down_2, a_w_in_2, a_q_gain_2, a_k_gain_2,
    a_w_out_2, b_w_in_2, b_q_gain_2, b_k_gain_2, b_sinks_2, b_w_out_2, c_w_in_2, c_q_a_gain_2,
    c_w_q_b_2, c_kv_a_gain_2, c_w_kv_b_2, c_q_gain_2, c_k_gain_2, c_w_out_2,
):
    x = first_block(
        x, norm_mix, w_in, fox_f_bias, gdn_conv_w, gdn_a_log, gdn_dt_bias, gdn_norm,
        w_branch_fox, w_branch_gdn, w_out, norm_ffn, w_up, ffn_conv_w, w_down, norm_final,
    )
    return second_block(
        x, positions_2, rel_bias_2, norm_mix_2, norm_mlp_2, w_up_2, w_down_2, a_w_in_2,
        a_q_gain_2, a_k_gain_2, a_w_out_2, b_w_in_2, b_q_gain_2, b_k_gain_2, b_sinks_2,
        b_w_out_2, c_w_in_2, c_q_a_gain_2, c_w_q_b_2, c_kv_a_gain_2, c_w_kv_b_2, c_q_gain_2,
        c_k_gain_2, c_w_out_2,
    )


_drawn_inputs = setup_inputs


def setup_inputs(seed=0):
    import zlib

    import numpy as np

    out = dict(_drawn_inputs(seed))
    spreads = {}
    factors = {'a_q_gain_2': 8.0,
     'a_k_gain_2': 8.0,
     'b_q_gain_2': 8.0,
     'b_k_gain_2': 8.0,
     'c_q_a_gain_2': 8.0,
     'c_kv_a_gain_2': 7.903,
     'c_q_gain_2': 8.0,
     'c_k_gain_2': 8.0}
    for name, (base, spread) in spreads.items():
        noise = np.random.default_rng([zlib.crc32(name.encode()), seed]).standard_normal(out[name].shape)
        drawn = base * np.exp(spread * noise) if base else spread * noise
        out[name] = __import__('jax').numpy.asarray(drawn.astype(out[name].dtype))
    for name, factor in factors.items():
        out[name] = (out[name] * factor).astype(out[name].dtype)
    return out
```

```python
from contextlib import ExitStack

import numpy as np
import concourse.bass as bass
from concourse import mybir

P = 128
F32 = mybir.dt.float32
F32R = mybir.dt.float32r
I32 = mybir.dt.int32
ALU = mybir.AluOpType
ACT = mybir.ActivationFunctionType
AX = mybir.AxisListType.X

S = 256
NT = S // P
D = 1024
KD = D // P
EPS = 1e-6
RAW, SPL = 8, 4
CHUNK = 1024
COLS = 512
SMALL = 704
NEG = -1.0e30
TAKEN = -3.0e38
H1 = 8
FF1, FF2 = 2816, 4096
AH = 16
TOPK = min(256, S // 4)
BUCKETS, MAX_DIST = 32, 128
ROPE, NOPE, QK3 = 32, 64, 96
SLOT = 2048


def bucket_ranges():
    half = BUCKETS // 2
    n = np.arange(S)
    large = half + (np.log(np.maximum(n, 1).astype(np.float32) / np.float32(half))
                    / np.float32(np.log(MAX_DIST / half)) * (BUCKETS - half)).astype(np.int32)
    b = np.where(n < half, n, np.minimum(large, BUCKETS - 1))
    return [(int(k), int(n[b == k][0]), int(n[b == k][-1]) + 1) for k in range(BUCKETS) if (b == k).any()]


class Chunk:

    def __init__(self, nk, w, pieces):
        self.nk, self.w, self.pieces = nk, w, pieces


def column_block(view, k_tiles, c0, w):
    nk = min(k_tiles, max(1, CHUNK // w))
    return [Chunk(min(nk, k_tiles - k), w, [(0, w, view[:, k:min(k + nk, k_tiles), c0:c0 + w])])
            for k in range(0, k_tiles, nk)]


def build(nc, x, norm_mix, w_in, fox_f_bias, gdn_conv_w, gdn_a_log, gdn_dt_bias, gdn_norm,
          w_branch_fox, w_branch_gdn, w_out, norm_ffn, w_up, ffn_conv_w, w_down, norm_final,
          positions_2, rel_bias_2, norm_mix_2, norm_mlp_2, w_up_2, w_down_2,
          a_w_in_2, a_q_gain_2, a_k_gain_2, a_w_out_2,
          b_w_in_2, b_q_gain_2, b_k_gain_2, b_sinks_2, b_w_out_2,
          c_w_in_2, c_q_a_gain_2, c_w_q_b_2, c_kv_a_gain_2, c_w_kv_b_2, c_q_gain_2, c_k_gain_2, c_w_out_2,
          out, layers=4):
    ctx = ExitStack()
    with ctx:
        def sb(name, shape, dt=F32):
            return ctx.enter_context(nc.sbuf_tensor("t_" + name, shape, dt))

        def psum(name, shape):
            return ctx.enter_context(nc.psum_tensor("p_" + name, shape, F32))

        sems = {}

        def sem(name):
            if name not in sems:
                sems[name] = ctx.enter_context(nc.semaphore("s_" + name))
            return sems[name]

        def rows(w):
            return w.rearrange("(k p) n -> p k n", p=P)

        raw = sb("raw", [P, RAW, CHUNK])
        wh = sb("wh", [P, SPL, CHUNK], F32R)
        wl = sb("wl", [P, SPL, CHUNK], F32R)
        X = sb("X", [P, NT, D])
        hTh = sb("hTh", [P, KD, S], F32R)
        hTl = sb("hTl", [P, KD, S], F32R)
        uTh = sb("uTh", [P, 4, S], F32R)
        uTl = sb("uTl", [P, 4, S], F32R)
        hid = sb("hid", [P, NT * COLS])
        A = sb("A", [P, 9 * SLOT])
        ident = sb("ident", [P, P])
        tri = sb("tri", [P, P])
        sgt = sb("sgt", [P, P])
        ones = sb("ones", [P, P])
        cmask = sb("cmask", [P, 3 * P])
        wmask = sb("wmask", [P, 3 * P])
        lvl = sb("lvl", [P, 7, P])
        gains = sb("gains", [P, 96])
        convw = sb("convw", [P, 96])
        fconvw = sb("fconvw", [P, 3, 44])
        rowc = sb("rowc", [P, 512])
        sm = sb("sm", [P, SMALL])
        mhalf = sb("mhalf", [P, 64])

        def slot(n, width=SLOT, off=0):
            return A[:, n * SLOT + off:n * SLOT + off + width]

        UP = psum("UP", [P, 2 * COLS])
        AC = psum("AC", [P, 4 * COLS])
        TP = psum("TP", [P, 2 * COLS])

        def up(t, w=COLS):
            return UP[:, t * COLS:t * COLS + w]

        def acc(n, w=COLS, off=0):
            return AC[:, n * COLS + off:n * COLS + off + w]

        def tpb(n, w=COLS, off=0):
            return TP[:, n * COLS + off:n * COLS + off + w]

        def bank(g, t, w=COLS):
            return up(t, w) if g % 2 == 0 else acc(t, w)

        small_top = [0]

        def small(n):
            small_top[0] += n
            assert small_top[0] <= SMALL
            return sm[:, small_top[0] - n:small_top[0]]

        bias_table = nc.dram_tensor("bias_table", [AH, 3 * P], F32).ap()

        row_src = []

        def gain_rows(view, n, half=False):
            first = sum(r[1] for r in row_src)
            row_src.append((view, n, half))
            return first

        fold = lambda v: v.rearrange("(a b) -> a b", b=P)
        g_mix = gain_rows(fold(norm_mix[0]), KD)
        g_ffn = gain_rows(fold(norm_ffn[0]), KD)
        g_mix2 = gain_rows(norm_mix_2.rearrange("l (a b) -> (l a) b", b=P), 4 * KD)
        g_mlp2 = gain_rows(norm_mlp_2.rearrange("l (a b) -> (l a) b", b=P), 4 * KD)
        g_cq = gain_rows(fold(c_q_a_gain_2[0]), 2)
        g_ckv = gain_rows(c_kv_a_gain_2, 1)
        g_aq = gain_rows(a_q_gain_2, 2, True)
        g_ak = gain_rows(a_k_gain_2, 2, True)
        g_bq = gain_rows(b_q_gain_2, 1, True)
        g_bk = gain_rows(b_k_gain_2, 1, True)
        g_c3 = gain_rows(c_q_gain_2[:, 0:64], 1, True)
        gain_rows(c_k_gain_2[:, 0:64], 1, True)
        n_gain_rows = sum(r[1] for r in row_src)
        stage1 = slot(8, P)
        stage2 = slot(8, P, P)
        stage0 = slot(8, P, 640)
        stage3 = slot(8, 3 * P, 2 * P).rearrange("p (i c) -> p i c", i=3)

        stage_rb = slot(8, BUCKETS, 1024)[0:AH, :]
        stage_bt = slot(8, 3 * P, 1024 + BUCKETS)[0:AH, :]

        rc_bias = rowc[:, 0:24]
        rc_alog = rowc[:, 24:32]
        rc_gdn = rowc[:, 32:160]
        rc_cq = rowc[:, 160:256]
        rc_ck = rowc[:, 256:352]
        rc_sink = rowc[:, 352:368]
        rc_freq = rowc[:, 368:384]

        w_in_v, b1 = rows(w_in[0]), D
        fox_q, fox_k, fox_v = 0, D, 2 * D
        ff0 = 3 * D
        gq0 = ff0 + H1
        ga0 = gq0 + 3 * D
        gz0 = ga0 + 2 * H1
        gate0 = gz0 + D
        items = []
        chunks = []

        def add_block(cs):
            items.append(("block", len(chunks), cs, sum(1 for i in items if i[0] == "block")))
            chunks.extend(cs)
            return len(items) - 1

        def two_blocks(view, c0, k_tiles=KD):
            return [add_block(column_block(view, k_tiles, c0 + j * COLS, COLS)) for j in range(2)]

        def add_ffn(f):
            if f == 0:
                wu, wd, ff, n = rows(w_up[0]), w_down[0], FF1, FF1 // 256
                up_chunks = lambda j: [
                    Chunk(2, COLS, [(h * 256, 256, wu[:, 2 * k:2 * k + 2, h * FF1 + j * 256:h * FF1 + j * 256 + 256])
                                    for h in range(2)]) for k in range(4)]
                dn_chunks = lambda j: [
                    Chunk(1, COLS, [(0, COLS, rows(wd)[:, 2 * j + k:2 * j + k + 1, b * COLS:(b + 1) * COLS])])
                    for k in range(2) for b in range(2)]
            else:
                wu, wd, n = rows(w_up_2[f - 1]), w_down_2[f - 1], FF2 // COLS
                up_chunks = lambda j: column_block(wu, KD, j * COLS, COLS)
                dn_chunks = lambda j: [
                    Chunk(2, COLS, [(0, COLS, rows(wd)[:, 4 * j + 2 * k:4 * j + 2 * k + 2, b * COLS:(b + 1) * COLS])])
                    for k in range(2) for b in range(2)]
            items.append(("ffn", len(chunks), f, n))
            chunks.extend(up_chunks(0))
            for j in range(n - 1):
                chunks.extend(up_chunks(j + 1))
                chunks.extend(dn_chunks(j))
            chunks.extend(dn_chunks(n - 1))
            return len(items) - 1

        blk_gqkv = [b for j in range(3) for b in two_blocks(w_in_v, gq0 + j * D)]
        blk_small = add_block([Chunk(KD, 24, [(0, 8, w_in_v[:, :, ff0:ff0 + 8]),
                                              (8, 16, w_in_v[:, :, ga0:ga0 + 16])])])
        blk_gz = two_blocks(w_in_v, gz0)
        blk_fqk = two_blocks(w_in_v, fox_q) + two_blocks(w_in_v, fox_k)
        blk_fv = two_blocks(w_in_v, fox_v)
        blk_gf = two_blocks(w_in_v, gate0)
        blk_gg = two_blocks(w_in_v, gate0 + D)
        blk_bg = two_blocks(rows(w_branch_gdn[0]), 0)
        blk_bf = two_blocks(rows(w_branch_fox[0]), 0)
        blk_wo = two_blocks(rows(w_out[0]), 0)
        it_ffn = [add_ffn(0)]
        layer_blocks = []
        for layer in range(layers):
            kind, n = layer % 3, layer // 3
            b = {}
            if kind == 0:
                v = rows(a_w_in_2[n])
                b["q"] = two_blocks(v, 0)
                b["qi"] = add_block(column_block(v, KD, 1152, 512))
                b["kv"] = add_block(column_block(v, KD, 1024, 128))
                b["kiw"] = add_block(column_block(v, KD, 1664, 72))
                b["out"] = two_blocks(rows(a_w_out_2[n]), 0)
            elif kind == 1:
                v = rows(b_w_in_2[n])
                b["q"] = two_blocks(v, 0)
                b["kv"] = add_block(column_block(v, KD, 1024, 512))
                b["out"] = two_blocks(rows(b_w_out_2[n]), 0)
            else:
                b["lat"] = add_block(column_block(rows(c_w_in_2[n]), KD, 0, 416))
                b["q"] = [add_block(column_block(rows(c_w_q_b_2[n]), 2, j * COLS, COLS)) for j in range(3)]
                b["kv"] = [add_block(column_block(rows(c_w_kv_b_2[n]), 1, j * COLS, COLS)) for j in range(4)]
                b["out"] = two_blocks(rows(c_w_out_2[n]), 0)
            layer_blocks.append(b)
            it_ffn.append(add_ffn(layer + 1))

        arrive, total = [], [0] * RAW
        for c, ch in enumerate(chunks):
            total[c % RAW] += 16 * len(ch.pieces)
            arrive.append(total[c % RAW])

        def gid(it):
            return items[it][3]

        def raw_in(c):
            return sem(f"raw_in_{c % RAW}")

        def raw_view(c, w=None):
            ch = chunks[c]
            return raw[:, c % RAW, 0:ch.nk * ch.w].rearrange("p (k n) -> p k n", k=ch.nk)

        def size(c):
            return chunks[c].nk * chunks[c].w

        high_done = sem("high_done")
        split_done = sem("split_done")
        spl_free = sem("spl_free")

        def blk_free(g):
            return sem(f"bank_pair_free_{g % 2}")

        def per_iteration(counts, c):
            return counts[c + 8] - counts[c]

        T_STAGES = []

        def add_t(src, gain):
            T_STAGES.append((src, gain))
            return len(T_STAGES) - 1

        Xv = X[:, :, :]
        tok = lambda n: slot(n).rearrange("p (t d) -> p t d", t=NT)
        O_GDN, O_FOX, Y_SUM = 4, 3, 2
        t_in1 = add_t(Xv, g_mix)
        t_gdn = add_t(tok(O_GDN), None)
        t_fox = add_t(tok(O_FOX), None)
        t_y = add_t(tok(Y_SUM), None)
        t_ffn = [add_t(Xv, g_ffn)]
        t_mix, t_att = [], []
        O_ATT = 0
        for layer in range(layers):
            t_mix.append(add_t(Xv, g_mix2 + KD * layer))
            t_att.append(add_t(tok(O_ATT), None))
            t_ffn.append(add_t(Xv, g_mlp2 + KD * layer))
        normed = [n for n, (_, g) in enumerate(T_STAGES) if g is not None]
        rms_order = [t_in1, t_ffn[0], "final"] + [n for n in normed if n > t_ffn[0]]
        t_ready = sem("t_ready")
        t_done = sem("t_done")
        t_high = sem("t_high")
        t_split = sem("t_split")
        ss_done = sem("ss_done")
        r_done = sem("r_done")
        ss = small(2)
        r_tok = small(2)

        it_n = [items[i][3] for i in it_ffn]
        it_base = [sum(it_n[:f]) for f in range(layers + 1)]
        hid_done = sem("hid_done")
        sq_done = sem("sq_done")
        ut_done = sem("ut_done")
        uh_done = sem("uh_done")
        ul_done = sem("ul_done")
        conv_step = sem("conv_step")
        gate_done = sem("gate_done")
        prod_done = sem("prod_done")

        fm_blocks = blk_gqkv + blk_fqk
        tk_done = sem("tk_done")
        ft_done = sem("ft_done")
        fm_done = sem("fm_done")
        silu_done = sem("silu_done")

        def tk(m):
            return slot(6, 1024, (m % 2) * 1024).rearrange("p (t n) -> p t n", t=NT)

        cores = []
        QF, KF, VF = 0, 1, 2
        feat = lambda n: slot(n).rearrange("p (h s) -> p h s", s=S)

        def fox_core():
            return dict(
                heads=H1, dv=P, scale=1.0,
                q=lambda h, t: feat(QF)[:, h, t * P:(t + 1) * P],
                k=lambda h: feat(KF)[:, h, :],
                v=lambda h, kt: tok(VF)[:, kt, h * P:(h + 1) * P],
                o=lambda h, t: tok(O_FOX)[:, t, h * P:(h + 1) * P])

        def a_core():
            def half(h):
                return slice(64 * (h % 2), 64 * (h % 2) + 64)
            kv = slot(2, 256).rearrange("p (t n) -> p t n", t=NT)
            return dict(
                heads=AH, dv=64, scale=64 ** -0.5,
                q=lambda h, t: feat(4)[half(h), h // 2, t * P:(t + 1) * P],
                k=lambda h: slot(3, S)[half(h), :],
                v=lambda h, kt: kv[:, kt, 64:128],
                o=lambda h, t: tok(O_ATT)[:, t, h * 64:(h + 1) * 64])

        def b_core():
            def half(h):
                return slice(64 * (h % 2), 64 * (h % 2) + 64)
            kv = slot(2, 1024).rearrange("p (t n) -> p t n", t=NT)
            return dict(
                heads=AH, dv=64, scale=64 ** -0.5, sink=True,
                q=lambda h, t: feat(4)[half(h), h // 2, t * P:(t + 1) * P],
                k=lambda h: slot(3, 1024).rearrange("p (g s) -> p g s", s=S)[half(h), h // 4, :],
                v=lambda h, kt: kv[:, kt, 256 + 64 * (h // 4):256 + 64 * (h // 4) + 64],
                o=lambda h, t: tok(O_ATT)[:, t, h * 64:(h + 1) * 64])

        MQ, MK = (2, 3), (4, 6)
        KV3 = A[:, 7 * SLOT:9 * SLOT].rearrange("p (t h e) -> p t h e", t=NT, e=128)

        def c_core():
            return dict(
                heads=AH, dv=64, scale=QK3 ** -0.5,
                q=lambda h, t: feat(MQ[h // 8])[0:QK3, h % 8, t * P:(t + 1) * P],
                k=lambda h: feat(MK[h // 8])[0:QK3, h % 8, :],
                v=lambda h, kt: KV3[:, kt, h, 64:128],
                o=lambda h, t: tok(O_ATT)[:, t, h * 64:(h + 1) * 64])

        core_list = [fox_core(), a_core(), b_core(), c_core(), a_core()]
        core_base = [sum(c["heads"] for c in core_list[:n]) for n in range(6)]
        LG = slot(5, 768).rearrange("p (b n) -> p b n", b=2)
        PTs = slot(5, 768, 768).rearrange("p (b n) -> p b n", b=2)
        BM = slot(6, 768).rearrange("p (b n) -> p b n", b=2)
        SC = slot(6, 384, 768)
        AM = slot(6, 384, 1152)
        BIAS = A[:, 7 * SLOT:9 * SLOT].rearrange("p (h s) -> p h s", s=S)
        LF = lambda h, t: BM[:, h % 2, t * P:(t + 1) * P]
        mx = small(2 * AH)
        esum = small(2 * AH)
        esink = small(2 * AH)
        mx_v, esum_v, es_v = (v.rearrange("p (t h) -> p t h", t=NT) for v in (mx, esum, esink))
        core_in = sem("core_in")
        bm_done = sem("bm_done")
        s_done = sem("s_done")
        lg_done = sem("lg_done")
        m_done = sem("m_done")
        p_done = sem("p_done")
        pt_done = sem("pt_done")
        pe_done = sem("pe_done")
        pv_done = sem("pv_done")
        o_done = sem("o_done")

        CQ, CK, CV, VP, DA, DT, TI, TT, MISC = 0, 1, 2, 3, 4, 5, 6, 7, 8
        unit = lambda n: slot(n).rearrange("p (u s) -> p u s", s=P)
        GATE = X[:, :, :].rearrange("p t (h e) -> p (t h) e", e=P)
        group = lambda n, g: slot(n)[:, g * COLS:(g + 1) * COLS]
        kdec = slot(CV, 1024).rearrange("p (h s) -> p h s", s=P)
        S1 = slot(CV, 1024, 1024).rearrange("p (h s) -> p h s", s=P)
        Bm = slot(MISC, 1024).rearrange("p (b n) -> p b n", b=2)
        Us = slot(TI).rearrange("p (u s) -> p u s", s=P)
        UTs = hid[:, :].rearrange("p (b n) -> p b n", b=2)
        gx = small(48).rearrange("p (t n) -> p t n", t=NT)
        ge = small(48).rearrange("p (t n) -> p t n", t=NT)
        gu = small(48).rearrange("p (t n) -> p t n", t=NT)
        gl = small(32).rearrange("p (t n) -> p t n", t=NT)
        beta = small(16).rearrange("p (t n) -> p t n", t=NT)
        lf = small(16).rearrange("p (t n) -> p t n", t=NT)
        gg = small(16).rearrange("p (t n) -> p t n", t=NT)
        gc = small(16)
        kd = small(8)
        eg = small(8)
        nbeg = small(8)
        nr = small(32)
        oss = small(16)

        lat_ss = small(4)
        hss = small(64)
        cs = small(64)
        posf = small(2)
        widx = small(16)
        ropek = small(64).rearrange("p (t n) -> p t n", t=NT)
        posi = sb("posi", [P, NT], I32)
        max8 = small(16)

        def upto(engine, name, value):
            engine.wait_ge(sem(name), value)

        def small_loads(sp):
            sp.dma_start(stage_rb, rel_bias_2.rearrange("b h -> h b"), allow_slow_non_contiguous=True).then_inc(sem("rel_in"), 16)
            for i in range(3):
                sp.dma_start(stage3[0:44, i, :], ffn_conv_w[0, i].rearrange("(a b) -> a b", b=P))\
                  .then_inc(sem("taps_in"), 16)
            sp.dma_start(stage2[0:96, :], gdn_conv_w[0].rearrange("i (a b) -> (i a) b", b=P))\
              .then_inc(sem("taps_in"), 16)
            for dst, src in ((rc_bias[:, 0:8], fox_f_bias[0]), (rc_bias[:, 8:16], gdn_dt_bias[0]),
                             (rc_alog, gdn_a_log[0]), (rc_gdn, gdn_norm[0]), (rc_cq, c_q_gain_2[0]),
                             (rc_ck, c_k_gain_2[0]), (rc_sink, b_sinks_2[0])):
                sp.dma_start(dst, src.partition_broadcast(P)).then_inc(sem("rowc_in"), 16)
            sp.dma_start(posi[:, :], positions_2[0].rearrange("(t p) -> p t", p=P), allow_slow_non_contiguous=True)\
              .then_inc(sem("rowc_in"), 16)

        def ready(engine, n, half=1):
            if n == t_in1:
                engine.wait_ge(sem("x_in"), 16)
            elif n == t_gdn:
                engine.wait_ge(t_ready, 1)
            elif n == t_fox:
                engine.wait_ge(o_done, core_base[1])
            elif n == t_y:
                engine.wait_ge(t_ready, 2 + half)
            elif n in t_mix:
                engine.wait_ge(t_ready, 4 + 2 * t_mix.index(n) + half)
            elif n in t_att:
                layer = t_att.index(n)
                engine.wait_ge(o_done, core_base[layer + 1] + AH // 2 * (half + 1))
            else:
                layer = t_ffn.index(n)
                evacuated(engine, (blk_wo if layer == 0 else layer_blocks[layer - 1]["out"])[half])

        def evacuated(engine, it):
            g = gid(it)
            engine.wait_ge(blk_free(g), g // 2 + 1)

        def item_chunks(it):
            kind, c0 = items[it][0:2]
            return range(c0, c0 + (len(items[it][2]) if kind == "block" else 4))

        def accumulated(engine, it):
            kind, c0 = items[it][0:2]
            engine.wait_ge(spl_free, c0 + (len(items[it][2]) if kind == "block" else 8 * items[it][3]))

        def rms_index(n):
            return rms_order.index(n)


        def delta_rule_act(act, A_, link, read_gate):
            upto(act, "g_pre", 1)
            A_(ge[:, :, 0:16], ge[:, :, 0:16], ACT.Exp, scale=-1.0)
            A_(rc_alog, rc_alog, ACT.Exp)
            A_(ge[:, :, 16:24], gx[:, :, 16:24], ACT.Exp, scale=-1.0).then_inc(sem("g_exp"), 1)
            act.wait_ge(silu_done, 6)
            act.wait_ge(ft_done, 6)
            A_(slot(6), slot(CQ), ACT.Square).then_inc(sem("sq_qk"), 1)
            A_(slot(7), slot(CK), ACT.Square).then_inc(sem("sq_qk"), 1)
            read_gate(0)
            upto(act, "g_one", 1)
            A_(gl, gu[:, :, 0:16], ACT.Ln).then_inc(sem("g_ln"), 1)
            read_gate(1)
            upto(act, "beta_done", 1)
            for g in range(4):
                upto(act, "vt_done", g + 1)
                for i in range(4):
                    t, h = divmod(4 * g + i, H1)
                    last = A_(unit(VP)[:, 4 * g + i, :], acc(g, P, i * P), ACT.Copy, scale=beta[:, t, h:h + 1])
                last.then_inc(sem("vp_done"), 1)
            upto(act, "gc_done", 1)
            A_(kd, gc[:, 8:16], ACT.Exp)
            A_(eg, gc[:, 0:8], ACT.Exp).then_inc(sem("g_eg"), 1)
            for g in range(4):
                upto(act, "rr_done", g + 1)
                A_(group(DA, g), up(g % 2), ACT.Exp)
                A_(group(DT, g), tpb(g % 2), ACT.Exp).then_inc(sem("de_done"), 1)
            act.wait_ge(sem("g_eg"), 1)
            for g in range(2):
                upto(act, "kt_done", g + 1)
                for i in range(4):
                    h = 4 * g + i
                    last = A_(kdec[:, h, :], tpb(g, P, i * P), ACT.Copy, scale=kd[:, h:h + 1])
                last.then_inc(sem("kc_done"), 1)
            for level in range(1, 7):
                for g in range(4):
                    upto(act, "iu_done", 4 * (level - 1) + g + 1)
                    A_(UTs[:, g % 2, :], up(g % 2), ACT.Copy).then_inc(sem("iuc_done"), 1)
            for g in range(2):
                upto(act, "pu_done", g + 1)
                A_(slot(TI, COLS, g * COLS), up(g), ACT.Copy).then_inc(sem("uc_done"), 1)
            for g in range(2):
                upto(act, "ps_done", g + 1)
                A_(slot(CV, COLS, 1024 + g * COLS), acc(g), ACT.Copy).then_inc(sem("sc_done"), 1)
            for g in range(2):
                upto(act, "po_done", g + 1)
                A_(slot(DA, COLS, g * COLS), acc(2 + g), ACT.Copy).then_inc(sem("oc_done"), 1)
            for g in range(2):
                upto(act, "pq_done", g + 1)
                for i in range(4):
                    h = 4 * g + i
                    last = A_(hid[:, h * P:(h + 1) * P], tpb(g, P, i * P), ACT.Copy, scale=eg[:, h:h + 1])
                last.then_inc(sem("qs_done"), 1)
            for g in range(2):
                upto(act, "pu_done", 2 + g + 1)
                A_(slot(TI, COLS, (2 + g) * COLS), acc(g), ACT.Copy).then_inc(sem("uc_done"), 1)

        LAT = slot(3, 832).rearrange("p (t n) -> p t n", t=NT)
        Q3 = A[:, 0:2 * 1536]
        Q3v = Q3.rearrange("p (t h e) -> p t h e", t=NT, e=QK3)
        W3 = A[:, 4 * SLOT:4 * SLOT + 3072]
        KSQ = slot(2).rearrange("p (n e) -> p n e", e=64)

        def latent_act(act, A_, link, b, read_block):
            read_block(b["lat"], lambda t: LAT[:, t, :], 416, r_tok)
            act.wait_ge(blk_free(gid(b["lat"])), gid(b["lat"]) // 2 + 1)
            n = 0
            for lo, hi in ((0, 256), (256, 384)):
                for t in range(NT):
                    last = A_(hid[:, n * 256:n * 256 + hi - lo], LAT[:, t, lo:hi], ACT.Square,
                              accum_out=lat_ss[:, n:n + 1])
                    n += 1
            last.then_inc(sem("ls_done"), 1)
            upto(act, "lt_done", 1)
            for k in range(3):
                gain = g_cq + k if k < 2 else g_ckv
                last = A_(uTh[:, k, :], TP[:, k * S:(k + 1) * S], ACT.Copy, scale=gains[:, gain:gain + 1])
            last.then_inc(sem("lh_done"), 1)
            upto(act, "lr_done", 1)
            for j in range(3):
                cols = lambda t: slice(t * 1536 + j * COLS, t * 1536 + (j + 1) * COLS)
                read_block(b["q"][j], lambda t: Q3[:, cols(t)], COLS, lat_ss[:, 0:2],
                           square=lambda t: (W3[:, cols(t)], bank(gid(b["q"][j]), t)))
            for j in range(4):
                read_block(b["kv"][j], lambda t: KV3[:, t, 4 * j:4 * j + 4, :].rearrange("p h e -> p (h e)"),
                           COLS, lat_ss[:, 2:4],
                           square=lambda t: (KSQ[:, 16 * t + 4 * j:16 * t + 4 * j + 4, :],
                                             bank(gid(b["kv"][j]), t).rearrange("p (h e) -> p h e", e=P)[:, :, 0:64]))
            for n in range(16):
                upto(act, "q3_done", n + 1)
                slots = MQ if n < 8 else MK
                i = n % 8
                dst = slot(slots[i // 4], COLS, (i % 4) * COLS)[0:QK3, :]
                col = g_c3 + n // 8
                A_(dst, (AC if n % 2 == 0 else TP)[0:QK3, 0:COLS], ACT.Copy, scale=gains[0:QK3, col:col + 1])\
                    .then_inc(sem("q3c_done"), 1)

        def delta_rule_dve(dve, V, link, ahead):
            evacuated(dve, blk_small)
            link(V.tensor_tensor(gx, gx, rc_bias.unsqueeze(1).broadcast_to([P, NT, 24]), ALU.add))
            V.scalar_tensor_tensor(ge[:, :, 0:16], gx[:, :, 0:16], -1.0, gx[:, :, 0:16], ALU.mult, ALU.max)\
             .then_inc(sem("g_pre"), 1)
            ahead(blk_gz[1])
            upto(dve, "g_exp", 1)
            V.tensor_scalar(gu, ge, 1.0, None, ALU.add).then_inc(sem("g_one"), 1)
            upto(dve, "g_one", 1)
            V.reciprocal(beta, gu[:, :, 16:24]).then_inc(sem("beta_done"), 1)
            e = ge[:, :, 0:16]
            link(V.scalar_tensor_tensor(e, gu[:, :, 0:16], 1.0, e, ALU.subtract, ALU.subtract))
            upto(dve, "g_ln", 1)
            link(V.reciprocal(gu[:, :, 0:16], gu[:, :, 0:16]))
            link(V.tensor_tensor(e, e, gu[:, :, 0:16], ALU.mult))
            link(V.tensor_tensor(e, gl, e, ALU.subtract))
            V.scalar_tensor_tensor(lf, gx[:, :, 0:8], 0.0, ge[:, :, 0:8], ALU.min, ALU.subtract)
            link(V.scalar_tensor_tensor(gg, gx[:, :, 8:16], 0.0, ge[:, :, 8:16], ALU.max, ALU.add))
            V.scalar_tensor_tensor(gg, gg, -1.0, rc_alog.unsqueeze(1).broadcast_to([P, NT, 8]),
                                   ALU.mult, ALU.mult).then_inc(sem("g_done"), 1)
            ahead(blk_gz[1] + 1)
            upto(dve, "gc_ps", 1)
            V.tensor_copy(gc, tpb(1, 16)).then_inc(sem("gc_done"), 1)
            upto(dve, "nr_ps", 1)
            V.tensor_scalar(nr, tpb(0, 32), EPS, None, ALU.add).then_inc(sem("nr_in"), 1)
            upto(dve, "g_eg", 1)
            link(V.scalar_tensor_tensor(nbeg, eg, -1.0, beta[:, 1, :], ALU.mult, ALU.mult))
            for g in range(4):
                if g >= 2:
                    upto(dve, "rr_done", g - 1)
                for i in range(4):
                    t, h = divmod(4 * g + i, H1)
                    last = V.tensor_scalar(hid[:, (g % 2) * COLS + i * P:(g % 2) * COLS + (i + 1) * P], sgt[:, :],
                                           gg[:, t, h:h + 1], None, ALU.mult)
                last.then_inc(sem("gs_done"), 1)
            for n in range(8):
                upto(dve, "rb_done", n + 1)
                which = CQ if n < 4 else CK
                part = slot(which, COLS, (n % 4) * COLS)
                V.scalar_tensor_tensor(part, part, P ** -0.5 if n < 4 else 1.0, acc(n % 4), ALU.mult, ALU.mult)\
                 .then_inc(sem("nn_done"), 1)
            for g in range(4):
                upto(dve, "kk_done", g + 1)
                upto(dve, "de_done", g + 1)
                for i in range(4):
                    u = 4 * g + i
                    t, h = divmod(u, H1)
                    v = unit(DA)[:, u, :]
                    last = V.scalar_tensor_tensor(v, acc(g, P, i * P), beta[:, t, h:h + 1], v, ALU.mult, ALU.mult)
                last.then_inc(sem("aa_done"), 1)
            for g in range(4):
                upto(dve, "qk_done", g + 1)
                V.tensor_tensor(group(DT, g), acc(g), group(DT, g), ALU.mult).then_inc(sem("at_done"), 1)
            eye = ident[:, :].unsqueeze(1).broadcast_to([P, 4, P])
            for g in range(4):
                upto(dve, "bt_done", g + 1)
                V.tensor_tensor(unit(TT)[:, 4 * g:4 * g + 4, :], eye,
                                up(g % 2).rearrange("p (u s) -> p u s", s=P), ALU.subtract)
                V.tensor_tensor(unit(TI)[:, 4 * g:4 * g + 4, :], eye,
                                Bm[:, g % 2, :].rearrange("p (u s) -> p u s", s=P), ALU.subtract)\
                 .then_inc(sem("t_upd"), 1)
            for level in range(1, 7):
                for g in range(4):
                    upto(dve, "ix_done", 4 * (level - 1) + g + 1)
                    upto(dve, "t_upd", 4 * level - 3 + g)
                    last = V.tensor_tensor(group(TT, g), group(TT, g), acc(2 * (g % 2)), ALU.subtract)
                    if level < 6:
                        last = V.tensor_tensor(group(TI, g), group(TI, g), acc(2 * (g % 2) + 1), ALU.subtract)
                    last.then_inc(sem("t_upd"), 1)
            for g in range(2):
                upto(dve, "pp_done", g + 1)
                for i in range(4):
                    h = 4 * g + i
                    v = unit(VP)[:, H1 + h, :]
                    last = V.scalar_tensor_tensor(v, up(g)[:, i * P:(i + 1) * P], nbeg[:, h:h + 1], v,
                                                  ALU.mult, ALU.add)
                last.then_inc(sem("r1_done"), 1)
            for g in range(2):
                upto(dve, "po_done", 2 + g + 1)
                upto(dve, "qs_done", g + 1)
                V.tensor_tensor(slot(DA, COLS, 1024 + g * COLS), acc(2 + g), hid[:, g * COLS:(g + 1) * COLS],
                                ALU.add).then_inc(sem("o1_done"), 1)

        def fox_scale(dve, V, m):
            dve.wait_ge(ft_done, m + 1)
            V.tensor_scalar(slot((m - 6) // 2, 1024, (m % 2) * 1024), TP[:, :], P ** -0.5 if m < 8 else 1.0,
                            None, ALU.mult).then_inc(fm_done, 1)

        def short_dve(dve, V, link, b, ahead, layer):
            kind, lb = layer % 3, layer // 3
            nk = 1 if kind == 0 else 4
            kv = slot(2, 256 if kind == 0 else 1024).rearrange("p (t n) -> p t n", t=NT)
            kiw = slot(2, 144, 256).rearrange("p (t n) -> p t n", t=NT)
            dup = slot(1, nk * 256, 1024).rearrange("p (t g d e) -> p t g d e", t=NT, g=nk, d=2) if kind == 0 else \
                slot(1, 1024).rearrange("p (t g d e) -> p t g d e", t=NT, g=nk, d=2)
            if layer in (0, 3):
                upto(dve, "bias_in", 16 * (1 if layer == 0 else 2))
                V.tensor_copy(BIAS, A[:, 3 * SLOT:5 * SLOT].rearrange("p (h s) -> p h s", s=S)[:, :, ::-1])\
                 .then_inc(sem("bias_copied"), 1)
                upto(dve, "bias_copied", 1 if layer == 0 else 2)
            for it in b["q"]:
                ahead(it + 1)
            for it in b["q"]:
                evacuated(dve, it)
            q32 = slot(0).rearrange("p (n e) -> p n e", e=64)
            sq = slot(3).rearrange("p (n e) -> p n e", e=64)
            link(V.tensor_tensor(slot(3), slot(0), slot(0), ALU.mult))
            link(V.tensor_reduce(hss[:, 0:32], sq, AX, ALU.add))
            V.tensor_scalar(hss[:, 0:32], hss[:, 0:32], 1.0 / 64, EPS, ALU.mult, ALU.add)\
             .then_inc(sem(f"hn_in_{layer}"), 1)
            rest_items = [b["qi"], b["kv"], b["kiw"]] if kind == 0 else [b["kv"]]
            for n, it in enumerate(rest_items):
                ahead(it + 1)
                if n == 0:
                    upto(dve, f"hn_done_{layer}", 1)
                    V.tensor_tensor(q32, q32, hss[:, 0:32].unsqueeze(2).broadcast_to([P, 32, 64]), ALU.mult)\
                     .then_inc(sem("qn_done"), 1)
            if kind == 0:
                evacuated(dve, b["kiw"])
                kid = slot(1, 256, 1280).rearrange("p (t d e) -> p t d e", t=NT, d=2)
                for t in range(NT):
                    V.tensor_copy(kid[:, t], kiw[:, t, 0:64].unsqueeze(1).broadcast_to([P, 2, 64]))
                last = V.tensor_scalar(widx.rearrange("p (t h) -> p t h", t=NT), kiw[:, :, 64:72], 8 ** -0.5, None,
                                       ALU.mult)
                last.then_inc(sem("kid_done"), 1)
            evacuated(dve, b["kv"])
            kk = kv[:, :, 0:64 * nk].rearrange("p t (g e) -> p t g e", e=64)
            ksq = slot(1, 128, 1536) if kind == 0 else slot(1, 512)
            ksq = ksq.rearrange("p (t g e) -> p t g e", t=NT, g=nk)
            link(V.tensor_tensor(ksq, kk, kk, ALU.mult))
            link(V.tensor_reduce(hss[:, 32:32 + 2 * nk], ksq.rearrange("p t g e -> p (t g) e"), AX, ALU.add))
            nh = 32 + 2 * nk
            V.tensor_scalar(hss[:, 32:nh], hss[:, 32:nh], 1.0 / 64, EPS, ALU.mult, ALU.add)\
             .then_inc(sem(f"hn_in_{layer}"), 1)
            upto(dve, f"hn_done_{layer}", 2)
            for t in range(NT):
                for g in range(nk):
                    n = 32 + t * nk + g
                    last = V.tensor_scalar(dup[:, t, g, :, :], kk[:, t, g, :].unsqueeze(1).broadcast_to([P, 2, 64]),
                                           hss[:, n:n + 1], None, ALU.mult)
            last.then_inc(sem(f"prep_done_{layer}"), 1)
            gk = g_ak + lb if kind == 0 else g_bk
            if kind == 0:
                upto(dve, "kit_ps", layer // 3 + 1)
                V.tensor_copy(slot(3, S, S), acc(0, S, S))
                V.tensor_copy(slot(3, 1024, 1024), UP[:, :]).then_inc(sem(f"kc_ps_{layer}"), 1)
                for h in range(8):
                    upto(dve, f"ir_done_{layer}", h + 1)
                    for t in range(NT):
                        cols = slice(0, P) if t == 0 else slice(P, 3 * P)
                        w = widx[:, 8 * t + h:8 * t + h + 1]
                        if h == 0:
                            last = V.tensor_scalar(SC[:, cols], LG[:, 0, cols], w, None, ALU.mult)
                        else:
                            last = V.scalar_tensor_tensor(SC[:, cols], LG[:, h % 2, cols], w, SC[:, cols],
                                                          ALU.mult, ALU.add)
                    last.then_inc(sem(f"ia_done_{layer}"), 1)
                    upto(dve, f"ia_done_{layer}", h + 1)
                link(V.tensor_tensor(SC, SC, cmask[:, :], ALU.add))
                for n in range(TOPK // 8):
                    if n == 2:
                        upto(dve, f"kt_ps_{layer}", 1)
                        V.tensor_scalar(slot(3, S), acc(0, S), gains[:, gk:gk + 1], None, ALU.mult)\
                         .then_inc(sem(f"kc_ps_{layer}"), 1)
                    for t in range(NT):
                        cols = slice(0, P) if t == 0 else slice(P, 3 * P)
                        last = V.max(max8[:, 8 * t:8 * t + 8], SC[:, cols])
                    link(last)
                    for t in range(NT):
                        cols = slice(0, P) if t == 0 else slice(P, 3 * P)
                        last = V.match_replace(SC[:, cols], max8[:, 8 * t:8 * t + 8], SC[:, cols], TAKEN)
                    link(last)
                link(V.tensor_scalar(AM, SC, -2.0e38, NEG, ALU.is_gt, ALU.mult))
                V.tensor_tensor(AM, AM, cmask[:, :], ALU.add).then_inc(sem(f"am_ready_{layer}"), 1)
            else:
                upto(dve, f"kt_ps_{layer}", 1)
                V.tensor_scalar(slot(3, 1024), UP[:, :], gains[:, gk:gk + 1], None, ALU.mult)\
                 .then_inc(sem(f"kc_ps_{layer}"), 1)

        def latent_dve(dve, V, link, b, ahead):
            ahead(b["lat"] + 1)
            evacuated(dve, b["lat"])
            csv = cs.rearrange("p (c t i) -> p c t i", c=2, t=NT)
            sin, cos = csv[:, 0], csv[:, 1]
            upto(dve, "cs_done", 1)
            kr = slot(6, 64).rearrange("p (t n) -> p t n", t=NT)
            k1 = slot(6, 128, 64).rearrange("p (a t i) -> p a t i", a=4, t=NT)
            krsq = slot(6, 64, 256).rearrange("p (t n) -> p t n", t=NT)
            krs = slot(6, 2, 384)
            V.tensor_tensor(krsq, LAT[:, :, 384:416], LAT[:, :, 384:416], ALU.mult)
            link(V.tensor_tensor(kr, LAT[:, :, 384:416], rc_ck[:, 64:96].unsqueeze(1).broadcast_to([P, NT, 32]),
                                 ALU.mult))
            V.tensor_reduce(krs, krsq, AX, ALU.add)
            V.tensor_tensor(k1[:, 0], kr[:, :, 0:16], cos, ALU.mult)
            V.tensor_tensor(k1[:, 1], kr[:, :, 16:32], sin, ALU.mult)
            V.tensor_tensor(k1[:, 2], kr[:, :, 16:32], cos, ALU.mult)
            link(V.tensor_tensor(k1[:, 3], kr[:, :, 0:16], sin, ALU.mult))
            V.tensor_tensor(ropek[:, :, 0:16], k1[:, 0], k1[:, 1], ALU.subtract)
            V.tensor_tensor(ropek[:, :, 16:32], k1[:, 2], k1[:, 3], ALU.add)
            upto(dve, "lh_done", 1)
            for k in range(3):
                gain = g_cq + k if k < 2 else g_ckv
                last = V.scalar_tensor_tensor(uTl[:, k, :], TP[:, k * S:(k + 1) * S], gains[:, gain:gain + 1],
                                              uTh[:, k, :].bitcast(F32), ALU.mult, ALU.subtract)
            last.then_inc(sem("ll_done"), 1)
            for it in b["q"] + b["kv"]:
                ahead(it + 1)
            for it in b["q"]:
                evacuated(dve, it)
            wide = lambda v: v.rearrange("p (n e) -> p n e", e=QK3)
            link(V.tensor_reduce(hss[:, 0:32], wide(W3), AX, ALU.add))
            V.tensor_scalar(hss[:, 0:32], hss[:, 0:32], 1.0 / QK3, EPS, ALU.mult, ALU.add).then_inc(sem("h3_in"), 1)
            for it in b["kv"]:
                evacuated(dve, it)
            knope = A[:, 7 * SLOT:9 * SLOT].rearrange("p (n e) -> p n e", e=P)[:, :, 0:64]
            link(V.tensor_reduce(hss[:, 32:64], KSQ, AX, ALU.add))
            for t in range(NT):
                last = V.tensor_scalar(hss[:, 32 + 16 * t:48 + 16 * t], hss[:, 32 + 16 * t:48 + 16 * t],
                                       krs[:, t:t + 1], None, ALU.add)
            link(last)
            V.tensor_scalar(hss[:, 32:64], hss[:, 32:64], 1.0 / QK3, EPS, ALU.mult, ALU.add).then_inc(sem("h3_in"), 1)
            upto(dve, "h3_done", 1)
            link(V.tensor_tensor(wide(Q3), wide(Q3), hss[:, 0:32].unsqueeze(2).broadcast_to([P, 32, QK3]), ALU.mult))
            link(V.tensor_tensor(wide(Q3)[:, :, 64:96], wide(Q3)[:, :, 64:96],
                                 rc_cq[:, 64:96].unsqueeze(1).broadcast_to([P, 32, 32]), ALU.mult))
            rot = slot(4).rearrange("p (a n i) -> p a n i", a=4, i=16)
            for t in range(NT):
                for a, (lo, f) in enumerate(((64, cos), (80, sin), (80, cos), (64, sin))):
                    last = V.tensor_tensor(rot[:, a, 16 * t:16 * t + 16, :], Q3v[:, t, :, lo:lo + 16],
                                           f[:, t, :].unsqueeze(1).broadcast_to([P, 16, 16]), ALU.mult)
            link(last)
            V.tensor_tensor(wide(Q3)[:, :, 64:80], rot[:, 0], rot[:, 1], ALU.subtract)
            V.tensor_tensor(wide(Q3)[:, :, 80:96], rot[:, 2], rot[:, 3], ALU.add).then_inc(sem("q3_ready"), 1)
            upto(dve, "h3_done", 2)
            upto(dve, "q3_done", 8)
            rk = hss[:, 32:64]
            V.tensor_tensor(wide(Q3)[:, :, 0:64], knope, rk.unsqueeze(2).broadcast_to([P, 32, 64]), ALU.mult)
            for t in range(NT):
                last = V.tensor_tensor(Q3v[:, t, :, 64:96], ropek[:, t, :].unsqueeze(1).broadcast_to([P, 16, 32]),
                                       rk[:, 16 * t:16 * t + 16].unsqueeze(2).broadcast_to([P, 16, 32]), ALU.mult)
            last.then_inc(sem("q3_ready"), 1)

        def delta_rule_pe(pe, M, transposes):
            cq = slot(CQ).rearrange("p (h s) -> p h s", s=S)
            ck = slot(CK).rearrange("p (h s) -> p h s", s=S)
            cv = slot(CV).rearrange("p (h s) -> p h s", s=S)
            tk_ = lambda v, h, t: v[:, h, t * P:(t + 1) * P]
            uh = lambda u: (u // H1, u % H1)
            upto(pe, "const_done", 1)
            upto(pe, "g_done", 1)
            pe.wait_ge(fm_done, 6)
            M(tpb(1, 8), tri[:, :], gg[:, 1, :], start=True, stop=True)
            M(tpb(1, 8, 8), sgt[:, :], gg[:, 0, :], start=True, stop=True).then_inc(sem("gc_ps"), 1)
            upto(pe, "sq_qk", 2)
            for n in range(32):
                which, h, t = n // 16, (n % 16) // 2, n % 2
                sq = slot(6 + which).rearrange("p (h s) -> p h s", s=S)
                last = M(tpb(0, 1, n), tk_(sq, h, t), ones[:, 0:1], start=True, stop=True)
            last.then_inc(sem("nr_ps"), 1)
            evacuated(pe, blk_gz[0])
            evacuated(pe, blk_gz[1])
            for g in range(4):
                transposes([(acc(g, P, i * P), tk_(cv, uh(4 * g + i)[1], uh(4 * g + i)[0])) for i in range(4)],
                           sem("vt_done"))
            upto(pe, "gc_done", 1)
            upto(pe, "nr_in", 1)
            for g in range(4):
                upto(pe, "gs_done", g + 1)
                if g >= 2:
                    upto(pe, "de_done", g - 1)
                for i in range(4):
                    behind = hid[:, (g % 2) * COLS + i * P:(g % 2) * COLS + (i + 1) * P]
                    M(up(g % 2)[:, i * P:(i + 1) * P], tri[:, :], behind, start=True, stop=True)
                    last = M(tpb(g % 2, P, i * P), behind, tri[:, :], start=True, stop=True)
                last.then_inc(sem("rr_done"), 1)
            upto(pe, "nr_done", 1)
            for n in range(8):
                if n < 4:
                    upto(pe, "vp_done", n + 1)
                else:
                    upto(pe, "nn_done", n - 3)
                for i in range(4):
                    col = 4 * n + i
                    last = M(acc(n % 4, P, i * P), nr[:, col:col + 1].broadcast_to([P, P]), ident[:, :],
                             start=True, stop=True)
                last.then_inc(sem("rb_done"), 1)
            upto(pe, "nn_done", 8)
            upto(pe, "de_done", 4)
            for g in range(2):
                transposes([(tpb(g, P, i * P), tk_(ck, 4 * g + i, 0)) for i in range(4)], sem("kt_done"))
            for g in range(4):
                for i in range(4):
                    t, h = uh(4 * g + i)
                    last = M(acc(g, P, i * P), tk_(ck, h, t), tk_(ck, h, t), start=True, stop=True)
                last.then_inc(sem("kk_done"), 1)
            for g in range(4):
                upto(pe, "aa_done", g + 1)
                for i in range(4):
                    t, h = uh(4 * g + i)
                    last = M(acc(g, P, i * P), tk_(ck, h, t), tk_(cq, h, t), start=True, stop=True)
                last.then_inc(sem("qk_done"), 1)
            for g in range(4):
                upto(pe, "b_done", g + 1)
                if g < 2:
                    upto(pe, "de_done", 3 + g)
                else:
                    upto(pe, "t_upd", g - 1)
                transposes([(up(g % 2)[:, i * P:(i + 1) * P], Bm[:, g % 2, i * P:(i + 1) * P]) for i in range(4)],
                           sem("bt_done"))

            def first_half(level, g):
                upto(pe, "b_done", 4 * level + g + 1)
                upto(pe, "t_upd", 4 * (level - 1) + g + 1)
                if level == 1 and g < 2:
                    upto(pe, "t_upd", 3 + g)
                for i in range(4):
                    last = M(up(g % 2)[:, i * P:(i + 1) * P], Bm[:, g % 2, i * P:(i + 1) * P],
                             unit(TT)[:, 4 * g + i, :], start=True, stop=True)
                last.then_inc(sem("iu_done"), 1)

            def second_half(level, g):
                upto(pe, "iuc_done", 4 * (level - 1) + g + 1)
                if level == 1 and g < 2:
                    upto(pe, "at_done", 4)
                else:
                    upto(pe, "t_upd", 4 * level + g - 1)
                for i in range(4):
                    ut = UTs[:, g % 2, i * P:(i + 1) * P]
                    last = M(acc(2 * (g % 2), P, i * P), unit(TI)[:, 4 * g + i, :], ut, start=True, stop=True)
                    if level < 6:
                        last = M(acc(2 * (g % 2) + 1, P, i * P), ut, unit(TI)[:, 4 * g + i, :], start=True, stop=True)
                last.then_inc(sem("ix_done"), 1)

            for level in range(1, 7):
                first_half(level, 0)
                first_half(level, 1)
                second_half(level, 0)
                first_half(level, 2)
                second_half(level, 1)
                first_half(level, 3)
                second_half(level, 2)
                second_half(level, 3)

            def heads(dst, lhs, rhs, signal):
                for g in range(2):
                    for i in range(4):
                        h = 4 * g + i
                        last = M(dst(g)[:, i * P:(i + 1) * P], lhs(h), rhs(h), start=True, stop=True)
                    last.then_inc(sem(signal), 1)

            upto(pe, "t_upd", 28)
            tt = unit(TT)
            heads(up, lambda h: tt[:, h, :], lambda h: unit(VP)[:, h, :], "pu_done")
            upto(pe, "uc_done", 2)
            upto(pe, "kc_done", 2)
            heads(acc, lambda h: kdec[:, h, :], lambda h: Us[:, h, :], "ps_done")
            upto(pe, "am_done", 4)
            heads(lambda g: acc(2 + g), lambda h: unit(DT)[:, h, :], lambda h: Us[:, h, :], "po_done")
            upto(pe, "sc_done", 2)
            heads(up, lambda h: tk_(ck, h, 1), lambda h: S1[:, h, :], "pp_done")
            heads(tpb, lambda h: tk_(cq, h, 1), lambda h: S1[:, h, :], "pq_done")
            upto(pe, "r1_done", 2)
            heads(acc, lambda h: tt[:, H1 + h, :], lambda h: unit(VP)[:, H1 + h, :], "pu_done")
            upto(pe, "uc_done", 4)
            upto(pe, "oc_done", 2)
            heads(lambda g: acc(2 + g), lambda h: unit(DT)[:, H1 + h, :], lambda h: Us[:, H1 + h, :], "po_done")

        def short_pe(pe, M, transposes, b, block_mm, layer):
            kind = layer % 3
            for it in b["q"] + ([b["qi"], b["kv"], b["kiw"]] if kind == 0 else [b["kv"]]):
                block_mm(it)
            def transpose_q():
                upto(pe, "qn_done", (0, 1, 3).index(layer) + 1)
                q = tok(0)
                for half in range(2):
                    dst, off = (TP, 0) if half == 0 else (AC, 2 * COLS)
                    transposes([(dst[:, off + k * S + t * P:off + k * S + (t + 1) * P],
                                 q[:, t, (4 * half + k) * P:(4 * half + k + 1) * P])
                                for k in range(4) for t in range(NT)], sem(f"qt_done_{layer}"))

            if kind == 1:
                transpose_q()
                upto(pe, f"prep_done_{layer}", 1)
            if kind == 0:
                for it in (b["qi"], b["kv"], b["kiw"]):
                    evacuated(pe, it)
                upto(pe, "kid_done", layer // 3 + 1)
                dup = slot(1, 512, 1024)
                qi = slot(1, 1024)
                transposes([(acc(0, P, (NT + t) * P), dup[:, (NT + t) * P:(NT + t + 1) * P]) for t in range(NT)] +
                           [(UP[:, k * S + t * P:k * S + (t + 1) * P], qi[:, t * COLS + k * P:t * COLS + (k + 1) * P])
                            for k in range(4) for t in range(NT)], sem("kit_ps"))
                upto(pe, f"kc_ps_{layer}", 1)
                QI = slot(3, 1024, 1024).rearrange("p (k s) -> p k s", s=S)
                KI = slot(3, S, S)
                for h in range(8):
                    if h >= 2:
                        upto(pe, f"ir_done_{layer}", h - 1)
                    part = slice(64 * (h % 2), 64 * (h % 2) + 64)
                    dst = up(h % 2, 3 * P)
                    M(dst[:, 0:P], QI[part, h // 2, 0:P], KI[part, 0:P], start=True, stop=True)
                    M(dst[:, P:3 * P], QI[part, h // 2, P:S], KI[part, :], start=True, stop=True)\
                        .then_inc(sem(f"is_done_{layer}"), 1)
                transpose_q()
                upto(pe, f"prep_done_{layer}", 1)
                transposes([(acc(0, P, t * P), dup[:, t * P:(t + 1) * P]) for t in range(NT)], sem(f"kt_ps_{layer}"))
                upto(pe, f"kc_ps_{layer}", 2)
            else:
                dup = slot(1, 1024).rearrange("p (t g e) -> p t g e", t=NT, g=4)
                evacuated(pe, b["kv"])
                transposes([(UP[:, g * S + t * P:g * S + (t + 1) * P], dup[:, t, g, :])
                            for g in range(4) for t in range(NT)], sem(f"kt_ps_{layer}"))
                upto(pe, f"kc_ps_{layer}", 1)
            upto(pe, f"qc_done_{layer}", 2)

        def latent_pe(pe, M, transposes, b, block_mm):
            block_mm(b["lat"])
            evacuated(pe, b["lat"])
            transposes([(TP[:, k * S + t * P:k * S + (t + 1) * P], LAT[:, t, k * P:(k + 1) * P])
                        for k in range(3) for t in range(NT)], sem("lt_done"))
            upto(pe, "ll_done", 1)
            for it in b["q"]:
                block_mm(it, uTh, uTl, 0)
            for it in b["kv"]:
                block_mm(it, uTh, uTl, 2)
            for it in b["kv"]:
                evacuated(pe, it)
            for n in range(16):
                if n % 8 == 0:
                    upto(pe, "q3_ready", n // 8 + 1)
                if n >= 2:
                    upto(pe, "q3c_done", n - 1)
                dst = AC if n % 2 == 0 else TP
                transposes([(dst[0:QK3, (i * NT + t) * P:(i * NT + t + 1) * P], Q3v[:, t, 2 * (n % 8) + i, :])
                            for i in range(2) for t in range(NT)], sem("q3_done"))
            upto(pe, "q3c_done", 16)

        block = ctx.enter_context(nc.Block())

        @block.sync
        def _(sp):
            sp.dma_start(Xv, x[0].rearrange("(t p) d -> p t d", p=P)).then_inc(sem("x_in"), 16)

            def load(c, j=None, it=0):
                if c >= RAW:
                    sp.wait_ge(split_done, c - RAW + 1 + (8 * it if j is not None else 0))
                for off, w, src in chunks[c].pieces:
                    dst = raw_view(c)[:, :, off:off + w]
                    sp.dma_start(dst, src).then_inc(raw_in(c), 16)

            def ffn_load(c, f, up_, k, it):
                sp.wait_ge(split_done, it * 8 + (c - RAW + 1))
                if f == 0 and up_:
                    wu = rows(w_up[0]).rearrange("p k (h n) -> p k h n", h=2)
                    for h in range(2):
                        sp.dma_start(raw_view(c)[:, :, h * 256:(h + 1) * 256],
                                     wu[:, 2 * k:2 * k + 2, h, bass.ds(it * 256 + 256, 256)]).then_inc(raw_in(c), 16)
                elif f == 0:
                    kk, b = divmod(k, 2)
                    wd = w_down[0].rearrange("(i k p) n -> p i k n", p=P, k=2)
                    sp.dma_start(raw_view(c), wd[:, bass.ds(it, 1), kk, b * COLS:(b + 1) * COLS]).then_inc(raw_in(c), 16)
                elif up_:
                    sp.dma_start(raw_view(c), rows(w_up_2[f - 1])[:, 2 * k:2 * k + 2,
                                                                 bass.ds(it * COLS + COLS, COLS)]).then_inc(raw_in(c), 16)
                else:
                    kk, b = divmod(k, 2)
                    wd = w_down_2[f - 1].rearrange("(i k p) n -> p i k n", p=P, k=2)
                    sp.dma_start(raw_view(c), wd[:, bass.ds(it * 2 + kk, 1), :, b * COLS:(b + 1) * COLS]
                                 .rearrange("p i k n -> p (i k) n")).then_inc(raw_in(c), 16)

            first = True
            for item in items:
                if item[0] == "block":
                    for c in range(item[1], item[1] + len(item[2])):
                        load(c)
                    if first:
                        first = False
                        small_loads(sp)
                        at = 0
                        for view, n, half in row_src[1:]:
                            for h in range(2 if half else 1):
                                dst = stage1[at:at + n, 64 * h:64 * h + 64] if half else stage1[at:at + n, :]
                                sp.dma_start(dst, view).then_inc(sem("rows_in"), 16)
                            at += n
                else:
                    _, c0, f, n = item
                    for k in range(4):
                        load(c0 + k)
                    with sp.Fori(0, n - 1) as it:
                        for k in range(4):
                            ffn_load(c0 + 4 + k, f, True, k, it)
                        for k in range(4):
                            ffn_load(c0 + 8 + k, f, False, k, it)
                    for k in range(4):
                        load(c0 + 4 + 8 * (n - 1) + k)
            upto(sp, "t_ready", 5 + 2 * layers)
            sp.dma_start(out[0].rearrange("(t p) d -> p t d", p=P), Xv).then_inc(sem("out_done"), 16)
            sp.wait_ge(sem("out_done"), 16)

        @block.scalar
        def _(act):
            A_ = act.activation
            chain = [0]

            def link(ins):
                chain[0] += 1
                ins.then_inc(sem("act_chain"), 1)
                act.wait_ge(sem("act_chain"), chain[0])

            def high(c, it=None):
                if it is None:
                    act.wait_ge(raw_in(c), arrive[c])
                    if c >= SPL:
                        act.wait_ge(spl_free, c - SPL + 1)
                else:
                    act.wait_ge(raw_in(c), it * per_iteration(arrive, c) + arrive[c])
                    act.wait_ge(spl_free, it * 8 + (c - SPL + 1))
                A_(wh[:, c % SPL, 0:size(c)], raw[:, c % RAW, 0:size(c)], ACT.Copy).then_inc(high_done, 1)

            def ahead(it):
                if it < len(items):
                    for c in item_chunks(it):
                        high(c)

            def read_block(it, dst, w, scale=None, func=ACT.Copy, square=None):
                ahead(it + 1)
                g = gid(it)
                accumulated(act, it)
                if square:
                    for t in range(NT):
                        to, src = square(t)
                        A_(to, src, ACT.Square, scale=scale[:, t:t + 1])
                for t in range(NT):
                    last = A_(dst(t), bank(g, t, w), func, scale=scale[:, t:t + 1])
                last.then_inc(blk_free(g), 1)

            def halves(n, j):
                return lambda t: tok(n)[:, t, j * COLS:(j + 1) * COLS]

            def sum_squares(q):
                for t in range(NT):
                    last = A_(hid[:, :], X[:, t, :], ACT.Square, accum_out=ss[:, t:t + 1])
                    if t == 0:
                        link(last)
                last.then_inc(ss_done, 1)

            def transpose_stage(n):
                gain = T_STAGES[n][1]
                for half in range(2):
                    act.wait_ge(t_done, 2 * n + half + 1)
                    src = TP[:, :] if half == 0 else AC[:, 2 * COLS:4 * COLS]
                    if gain is None:
                        last = A_(hTh[:, 4 * half:4 * half + 4, :], src.rearrange("p (k s) -> p k s", s=S), ACT.Copy)
                    else:
                        for k in range(4):
                            kk = 4 * half + k
                            last = A_(hTh[:, kk, :], src[:, k * S:(k + 1) * S], ACT.Copy,
                                      scale=gains[:, gain + kk:gain + kk + 1])
                    last.then_inc(t_high, 1)
                if gain is not None:
                    ready(act, n)
                    sum_squares(rms_index(n))
                    act.wait_ge(r_done, rms_index(n) + 1)

            def core(n):
                c = core_list[n]
                h0 = core_base[n]
                for i in range(c["heads"] + 1):
                    if i < c["heads"]:
                        act.wait_ge(m_done, h0 + i + 1)
                        for t in range(NT):
                            cols = LG[:, i % 2, 0:P] if t == 0 else LG[:, i % 2, P:3 * P]
                            k = t * AH + i
                            last = A_(cols, cols, ACT.Exp, bias=mx[:, k:k + 1], accum_out=esum[:, k:k + 1])
                        if c.get("sink"):
                            last = A_(es_v[:, :, i], es_v[:, :, i], ACT.Exp)
                        last.then_inc(p_done, 1)
                    if i >= 1:
                        act.wait_ge(pt_done, h0 + i)
                        A_(PTs[:, (i - 1) % 2, :], tpb((i - 1) % 2, 3 * P), ACT.Copy).then_inc(pe_done, 1)

            def ffn(f, it):
                n, b = it_n[f], it_base[f]
                c0 = items[it][1]
                squared = f > 0

                def body(j, used, nxt):
                    act.wait_ge(spl_free, used)
                    dn = c0 + 8 if nxt else c0 + 8 * (n - 1) + 4
                    for t in range(NT):
                        last = A_(hid[:, t * COLS:(t + 1) * COLS], up(t), ACT.Relu if squared else ACT.Copy,
                                  scale=r_tok[:, t:t + 1])
                    last.then_inc(hid_done, 1)
                    if nxt:
                        for k in range(4):
                            high(c0 + 4 + k, j)
                    if squared:
                        act.wait_ge(ut_done, j + (b + 1))
                        A_(uTh[:, :, :], TP[:, :].rearrange("p (k s) -> p k s", s=S), ACT.Copy).then_inc(uh_done, 1)
                    else:
                        act.wait_ge(conv_step, j * 3 + 3 * (b + 1))
                        A_(slot(0, 512), slot(0, 512), ACT.Silu).then_inc(gate_done, 1)
                        act.wait_ge(prod_done, j + (b + 1))
                        A_(uTh[:, 0:2, :], slot(1, 512).rearrange("p (k s) -> p k s", s=S), ACT.Copy)\
                            .then_inc(uh_done, 1)
                    for k in range(4):
                        if nxt:
                            high(dn + k, j)
                        else:
                            high(dn + k)

                body(0, c0 + 4, True)
                with act.Fori(1, n - 1) as j:
                    body(j, j * 8 + c0, True)
                body(n - 1, c0 + 8 * (n - 1), False)

            act.dma_start(stage0[0:KD, :], row_src[0][0]).then_inc(sem("mix_in"), 16)
            ahead(0)
            upto(act, "gains_done", 1)
            transpose_stage(t_in1)

            def feature_block(m):
                if m >= 2:
                    act.wait_ge(ft_done, m - 1)
                read_block(fm_blocks[m], lambda t: tk(m)[:, t, :], COLS, r_tok)

            def silu(m):
                act.wait_ge(fm_done, m + 1)
                part = slot(m // 2, 1024, (m % 2) * 1024)
                A_(part, part, ACT.Silu).then_inc(silu_done, 1)

            for m in range(6):
                feature_block(m)
                if m == 0:
                    upto(act, "angle_done", 1)
                    A_(cs, cs, ACT.Sin).then_inc(sem("cs_done"), 1)
                else:
                    silu(m - 1)
            read_block(blk_small, lambda t: gx[:, t, :], 24, r_tok)
            silu(5)
            delta_rule_act(act, A_, link, lambda j: read_block(
                blk_gz[j], lambda t: X[:, t, j * COLS:(j + 1) * COLS], COLS, r_tok, ACT.Silu))
            upto(act, "o1_done", 2)
            for u in range(16):
                last = A_(unit(DT)[:, 0, :] if u % 2 == 0 else unit(DT)[:, 1, :], unit(DA)[:, u, :], ACT.Square,
                          accum_out=oss[:, u:u + 1])
                if u < 15:
                    link(last)
            last.then_inc(sem("oss_done"), 1)
            for m in range(6, 10):
                feature_block(m)
            for j in range(2):
                read_block(blk_fv[j], halves(VF, j), COLS, r_tok)
            core(0)
            for j in range(2):
                if j == 0:
                    act.wait_ge(o_done, core_base[1])
                read_block(blk_gf[j], halves(0, j), COLS, r_tok, ACT.Sigmoid)
            for j in range(2):
                read_block(blk_gg[j], halves(1, j), COLS, r_tok, ACT.Sigmoid)
            for st, blocks in ((t_gdn, blk_bg), (t_fox, blk_bf), (t_y, blk_wo)):
                transpose_stage(st)
                for it in blocks:
                    ahead(it + 1)
            transpose_stage(t_ffn[0])
            ffn(0, it_ffn[0])
            ahead(it_ffn[0] + 1)
            upto(act, "xf_done", 2)
            sum_squares(2)

            for layer in range(layers):
                b, kind, lb = layer_blocks[layer], layer % 3, layer // 3
                transpose_stage(t_mix[layer])
                if kind == 2:
                    latent_act(act, A_, link, b, read_block)
                else:
                    for j in range(2):
                        read_block(b["q"][j], halves(0, j), COLS, r_tok)
                    if kind == 0:
                        read_block(b["qi"], lambda t: slot(1, 1024)[:, t * COLS:(t + 1) * COLS], COLS, r_tok)
                        read_block(b["kv"], lambda t: slot(2, 256)[:, t * P:(t + 1) * P], P, r_tok)
                        read_block(b["kiw"], lambda t: slot(2, 144, 256)[:, t * 72:(t + 1) * 72], 72, r_tok)
                    else:
                        read_block(b["kv"], lambda t: slot(2, 1024)[:, t * COLS:(t + 1) * COLS], COLS, r_tok)
                    if kind == 0:
                        for h in range(8):
                            upto(act, f"is_done_{layer}", h + 1)
                            if h >= 2:
                                upto(act, f"ia_done_{layer}", h - 1)
                            A_(LG[:, h % 2, :], up(h % 2, 3 * P), ACT.Relu, scale=0.125)\
                                .then_inc(sem(f"ir_done_{layer}"), 1)
                    gq = g_aq + lb if kind == 0 else g_bq
                    for half in range(2):
                        upto(act, f"qt_done_{layer}", half + 1)
                        src = TP[:, :] if half == 0 else AC[:, 2 * COLS:4 * COLS]
                        A_(slot(4, 1024, 1024 * half), src, ACT.Copy, scale=gains[:, gq:gq + 1])\
                            .then_inc(sem(f"qc_done_{layer}"), 1)
                core(layer + 1)
                transpose_stage(t_att[layer])
                for it in b["out"]:
                    ahead(it + 1)
                transpose_stage(t_ffn[layer + 1])
                ffn(layer + 1, it_ffn[layer + 1])
                ahead(it_ffn[layer + 1] + 1)

        @block.gpsimd
        def _(pool):
            chain = [0]

            def link(ins):
                chain[0] += 1
                ins.then_inc(sem("pool_chain"), 1)
                pool.wait_ge(sem("pool_chain"), chain[0])

            def select(view, base, pattern, cm, fill, op=ALU.is_ge):
                link(pool.affine_select(out=view, in_=view, compare_op=op, fill=fill, base=base,
                                        pattern=pattern, channel_multiplier=cm))

            pool.memset(mhalf[:, :], -0.5)
            pool.memset(ones[:, :], 1.0)
            pool.memset(rc_bias[:, 16:24], 0.0)
            inv_freq = (np.float32(10000.0) ** (-np.arange(0, ROPE, 2, dtype=np.float32) / np.float32(ROPE)))
            for i, f in enumerate(inv_freq):
                pool.memset(rc_freq[:, i:i + 1], float(np.float32(f)))
            pool.memset(ident[:, :], 0.0)
            pool.memset(tri[:, :], 1.0)
            pool.memset(sgt[:, :], 1.0)
            pool.memset(cmask[:, :], 0.0)
            pool.memset(wmask[:, :], 0.0)
            link(pool.memset(lvl[:, :, :], 0.0))
            select(ident[:, :], 0, [[-1, P]], 1, 1.0, ALU.not_equal)
            pool.wait_ge(sem("pool_chain"), chain[0])
            pool.nop().then_inc(sem("ident_done"), 1)
            select(tri[:, :], 0, [[1, P]], -1, 0.0)
            select(sgt[:, :], -1, [[-1, P]], 1, 0.0)
            for m in (cmask, wmask):
                select(m[:, 0:P], 0, [[-1, P]], 1, NEG)
                select(m[:, P:3 * P], P, [[-1, 2 * P]], 1, NEG)
            select(wmask[:, P:3 * P], -1, [[1, 2 * P]], -1, NEG)
            for l in range(7):
                w = 1 << l
                n = P // (2 * w)
                view = lvl[:, l, :].rearrange("p (i r) -> p i r", r=2 * w)[:, :, 0:w]
                link(pool.memset(view, 1.0))
                select(view, -w, [[-2 * w, n], [0, w]], 1, 0.0)
                select(view, 2 * w - 1, [[2 * w, n], [0, w]], -1, 0.0)
            pool.nop().then_inc(sem("const_done"), 1)

            def rms(q):
                pool.wait_ge(ss_done, q + 1)
                link(pool.tensor_scalar(r_tok, ss, 1.0 / D, EPS, ALU.mult, ALU.add))
                pool.tensor_tensor(r_tok, r_tok, mhalf[:, 0:NT], ALU.pow).then_inc(r_done, 1)

            rms(0)
            pool.wait_ge(sem("rel_built"), 1)
            pool.dma_start(bias_table, stage_bt).then_inc(sem("bias_out"), 16)
            upto(pool, "nr_in", 1)
            pool.tensor_tensor(nr, nr, mhalf[:, 0:32], ALU.pow).then_inc(sem("nr_done"), 1)
            idx = 0
            for level in range(7):
                for g in range(4):
                    if level == 0:
                        upto(pool, "aa_done", g + 1)
                    if idx >= 2:
                        if idx - 2 < 4:
                            upto(pool, "t_upd", idx - 1)
                        else:
                            upto(pool, "iu_done", idx - 5)
                    pool.tensor_tensor(Bm[:, g % 2, :].rearrange("p (u s) -> p u s", s=P),
                                       unit(DA)[:, 4 * g:4 * g + 4, :],
                                       lvl[:, level, :].unsqueeze(1).broadcast_to([P, 4, P]),
                                       ALU.mult).then_inc(sem("b_done"), 1)
                    idx += 1
                if level == 0:
                    for g in range(4):
                        upto(pool, "at_done", g + 1)
                        v = unit(DT)[:, 4 * g:4 * g + 4, :]
                        pool.tensor_tensor(v, v, tri[:, :].unsqueeze(1).broadcast_to([P, 4, P]), ALU.mult)\
                            .then_inc(sem("am_done"), 1)
            for j in range(2):
                evacuated(pool, blk_gz[j])
            pool.tensor_tensor(GATE, GATE, rc_gdn.unsqueeze(1).broadcast_to([P, 16, P]), ALU.mult)\
                .then_inc(sem("gz_done"), 1)
            upto(pool, "oss_done", 1)
            link(pool.tensor_scalar(oss, oss, 1.0 / P, EPS, ALU.mult, ALU.add))
            pool.tensor_tensor(oss, oss, mhalf[:, 0:16], ALU.pow).then_inc(sem("ro_done"), 1)

            def load_bias(n):
                skew = bass.AP(bias_table.tensor, 0, [[1, P], [3 * P, AH], [1, S]])
                pool.dma_start(A[:, 3 * SLOT:5 * SLOT].rearrange("p (h s) -> p h s", s=S), skew)\
                    .then_inc(sem("bias_in"), 16)

            pool.wait_ge(t_ready, 1)
            pool.dma_start(Xv, x[0].rearrange("(t p) d -> p t d", p=P)).then_inc(sem("x_again"), 16)
            pool.wait_ge(t_split, 2 * t_y + 2)
            pool.wait_ge(sem("bias_out"), 16)
            load_bias(0)
            pool.dma_start(slot(2, D), norm_final.partition_broadcast(P)).then_inc(sem("nf_in"), 16)
            rms(1)
            rms(2)
            bm = 0
            for layer in range(layers):
                kind = layer % 3
                rms(rms_index(t_mix[layer]))
                if kind == 2:
                    upto(pool, "ls_done", 1)
                    pool.tensor_scalar(lat_ss[:, 0:2], lat_ss[:, 0:2], 1.0 / 256, EPS, ALU.mult, ALU.add)
                    link(pool.tensor_scalar(lat_ss[:, 2:4], lat_ss[:, 2:4], 1.0 / 128, EPS, ALU.mult, ALU.add))
                    pool.tensor_tensor(lat_ss, lat_ss, mhalf[:, 0:4], ALU.pow).then_inc(sem("lr_done"), 1)
                    for n in range(2):
                        upto(pool, "h3_in", n + 1)
                        pool.tensor_tensor(hss[:, 32 * n:32 * n + 32], hss[:, 32 * n:32 * n + 32], mhalf[:, 0:32],
                                           ALU.pow).then_inc(sem("h3_done"), 1)
                else:
                    nh = 34 if kind == 0 else 40
                    for n, (lo, hi) in enumerate(((0, 32), (32, nh))):
                        upto(pool, f"hn_in_{layer}", n + 1)
                        pool.tensor_tensor(hss[:, lo:hi], hss[:, lo:hi], mhalf[:, 0:hi - lo], ALU.pow)\
                            .then_inc(sem(f"hn_done_{layer}"), 1)
                    h0 = core_base[layer + 1]
                    if kind == 0:
                        upto(pool, f"am_ready_{layer}", 1)
                    else:
                        upto(pool, "bias_copied", 1)
                        upto(pool, f"kc_ps_{layer}", 1)
                    mask = AM if kind == 0 else wmask[:, :]
                    for h in range(AH):
                        if h >= 2:
                            pool.wait_ge(lg_done, h0 + h - 1)
                        pool.tensor_tensor(BM[:, h % 2, 0:P], BIAS[:, h, P:S], mask[:, 0:P], ALU.add)
                        pool.tensor_tensor(BM[:, h % 2, P:3 * P], BIAS[:, h, :], mask[:, P:3 * P], ALU.add)\
                            .then_inc(bm_done, 1)
                if layer == 2:
                    pool.wait_ge(o_done, core_base[4])
                    load_bias(1)
                rms(rms_index(t_ffn[layer + 1]))
                b0, n = it_base[layer + 1], it_n[layer + 1]
                with pool.Fori(0, n) as j:
                    pool.wait_ge(hid_done, j + (b0 + 1))
                    pool.tensor_tensor(hid[:, :], hid[:, :], hid[:, :], ALU.mult).then_inc(sq_done, 1)

        @block.vector
        def _(dve):
            V = dve
            chain = [0]

            def link(ins):
                chain[0] += 1
                ins.then_inc(sem("dve_chain"), 1)
                dve.wait_ge(sem("dve_chain"), chain[0])

            def rest(c, it=None):
                dve.wait_ge(high_done, c + 1 if it is None else it * 8 + (c + 1))
                n = size(c)
                V.tensor_tensor(wl[:, c % SPL, 0:n], raw[:, c % RAW, 0:n], wh[:, c % SPL, 0:n].bitcast(F32),
                                ALU.subtract).then_inc(split_done, 1)

            def ahead(it):
                if it < len(items):
                    for c in item_chunks(it):
                        rest(c)

            def transpose_stage(n):
                gain = T_STAGES[n][1]
                for half in range(2):
                    dve.wait_ge(t_high, 2 * n + half + 1)
                    src = TP[:, :] if half == 0 else AC[:, 2 * COLS:4 * COLS]
                    hi = hTh[:, 4 * half:4 * half + 4, :].bitcast(F32)
                    if gain is None:
                        last = V.tensor_tensor(hTl[:, 4 * half:4 * half + 4, :],
                                               src.rearrange("p (k s) -> p k s", s=S), hi, ALU.subtract)
                    else:
                        for k in range(4):
                            kk = 4 * half + k
                            last = V.scalar_tensor_tensor(hTl[:, kk, :], src[:, k * S:(k + 1) * S],
                                                          gains[:, gain + kk:gain + kk + 1],
                                                          hTh[:, kk, :].bitcast(F32), ALU.mult, ALU.subtract)
                    last.then_inc(t_split, 1)

            def core(n):
                c = core_list[n]
                h0 = core_base[n]
                bm0 = {1: 0, 2: AH, 4: 2 * AH}.get(n)

                def gates_behind(h):
                    for t in range(NT):
                        last = V.tensor_scalar(LF(h, t), sgt[:, :], lf[:, t, h:h + 1], None, ALU.mult)
                    last.then_inc(sem("lf_done"), 1)

                if n == 0:
                    gates_behind(0)
                    gates_behind(1)
                for i in range(c["heads"] + 2):
                    if i < c["heads"]:
                        if n in (0, 3):
                            mask = cmask[:, :]
                        else:
                            mask = BM[:, i % 2, :]
                            dve.wait_ge(bm_done, bm0 + i + 1)
                        dve.wait_ge(s_done, h0 + i + 1)
                        V.scalar_tensor_tensor(LG[:, i % 2, :], acc(2 + i % 2, 3 * P), c["scale"], mask,
                                               ALU.mult, ALU.add).then_inc(lg_done, 1)
                        if n == 0 and i + 2 < c["heads"]:
                            gates_behind(i + 2)
                        dve.wait_ge(lg_done, h0 + i + 1)
                        V.tensor_reduce(mx[:, i:i + 1], LG[:, i % 2, 0:P], AX, ALU.max)
                        link(V.tensor_reduce(mx[:, AH + i:AH + i + 1], LG[:, i % 2, P:3 * P], AX, ALU.max))
                        if c.get("sink"):
                            link(V.tensor_scalar(mx_v[:, :, i], mx_v[:, :, i], rc_sink[:, i:i + 1], -1.0,
                                                 ALU.max, ALU.mult))
                            V.tensor_scalar(es_v[:, :, i], mx_v[:, :, i], rc_sink[:, i:i + 1], None, ALU.add)\
                             .then_inc(m_done, 1)
                        else:
                            V.tensor_scalar(mx_v[:, :, i], mx_v[:, :, i], -1.0, None, ALU.mult).then_inc(m_done, 1)
                    if i >= 2:
                        h = i - 2
                        dve.wait_ge(p_done, h0 + h + 1)
                        if c.get("sink"):
                            link(V.tensor_tensor(esum_v[:, :, h], esum_v[:, :, h], es_v[:, :, h], ALU.add))
                        link(V.reciprocal(esum_v[:, :, h], esum_v[:, :, h]))
                        dve.wait_ge(pv_done, h0 + h + 1)
                        for t in range(NT):
                            last = V.tensor_scalar(c["o"](h, t), acc(h % 2, c["dv"], t * P),
                                                   esum[:, t * AH + h:t * AH + h + 1], None, ALU.mult)
                        last.then_inc(o_done, 1)
                dve.wait_ge(o_done, h0 + c["heads"])

            def ffn(f, it):
                n, b = it_n[f], it_base[f]
                c0 = items[it][1]
                cv = slot(0, 1024).rearrange("p (k s) -> p k s", s=S)
                fc = fconvw[:, :, :]

                def conv(j, static):
                    def w(tap, k):
                        tile = (k // 2) * 22 + k % 2
                        if static is None:
                            return fc[:, tap, bass.ds(j * 2 + tile, 1)]
                        return fc[:, tap, 2 * static + tile:2 * static + tile + 1]
                    dve.wait_ge(ut_done, j + (b + 1))
                    for tap in (2, 1, 0):
                        d = 2 - tap
                        for k in range(4):
                            src = TP[:, k * S:(k + 1) * S - d]
                            if tap == 2:
                                last = V.tensor_scalar(cv[:, k, :], src, w(tap, k), None, ALU.mult)
                            else:
                                last = V.scalar_tensor_tensor(cv[:, k, d:S], src, w(tap, k), cv[:, k, d:S],
                                                              ALU.mult, ALU.add)
                        last.then_inc(conv_step, 1)
                        dve.wait_ge(conv_step, j * 3 + (3 * b + 3 - tap))

                def body(j, nxt):
                    if nxt:
                        for k in range(4):
                            rest(c0 + 4 + k, j)
                    if f > 0:
                        dve.wait_ge(uh_done, j + (b + 1))
                        V.tensor_tensor(uTl[:, :, :], TP[:, :].rearrange("p (k s) -> p k s", s=S),
                                        uTh[:, :, :].bitcast(F32), ALU.subtract).then_inc(ul_done, 1)
                    else:
                        conv(j, None if nxt else n - 1)
                        dve.wait_ge(gate_done, j + (b + 1))
                        V.tensor_tensor(slot(1, 512), slot(0, 512), slot(0, 512, 512), ALU.mult).then_inc(prod_done, 1)
                        dve.wait_ge(prod_done, j + (b + 1))
                        dve.wait_ge(uh_done, j + (b + 1))
                        V.tensor_tensor(uTl[:, 0:2, :], slot(1, 512).rearrange("p (k s) -> p k s", s=S),
                                        uTh[:, 0:2, :].bitcast(F32), ALU.subtract).then_inc(ul_done, 1)
                    for k in range(4):
                        if nxt:
                            rest(c0 + 8 + k, j)
                        else:
                            rest(c0 + 8 * (n - 1) + 4 + k)

                with dve.Fori(0, n - 1) as j:
                    body(j, True)
                body(n - 1, False)

            def add_to_x(signal):
                for cb in range(2):
                    for t in range(NT):
                        last = V.tensor_tensor(X[:, t, cb * COLS:(cb + 1) * COLS],
                                               X[:, t, cb * COLS:(cb + 1) * COLS], acc(2 * t + cb), ALU.add)
                    last.then_inc(signal, 1)

            def residual_blocks(blocks, last_signal=None):
                for j, it in enumerate(blocks):
                    ahead(it + 1)
                    g = gid(it)
                    accumulated(dve, it)
                    for t in range(NT):
                        v = X[:, t, j * COLS:(j + 1) * COLS]
                        last = V.tensor_tensor(v, v, bank(g, t), ALU.add)
                    last.then_inc(blk_free(g), 1)

            upto(dve, "gt_done", 1)
            V.tensor_copy(gains[:, 0:KD], up(0, KD)).then_inc(sem("gains_done"), 1)
            upto(dve, "gains_done", 1)
            ahead(0)
            transpose_stage(t_in1)

            def conv4(m):
                dve.wait_ge(ft_done, m + 1)
                dst = slot(m // 2, 1024, (m % 2) * 1024).rearrange("p (k s) -> p k s", s=S)
                for tap in (3, 2, 1, 0):
                    d = 3 - tap
                    for k in range(4):
                        w = convw[:, tap * 24 + 4 * m + k:tap * 24 + 4 * m + k + 1]
                        src = TP[:, k * S:(k + 1) * S - d]
                        if tap == 3:
                            last = V.tensor_scalar(dst[:, k, :], src, w, None, ALU.mult)
                        else:
                            last = V.scalar_tensor_tensor(dst[:, k, d:S], src, w, dst[:, k, d:S], ALU.mult, ALU.add)
                    if tap:
                        link(last)
                last.then_inc(fm_done, 1)

            ahead(fm_blocks[1])
            upto(dve, "taps_ps", 1)
            V.tensor_copy(convw[:, :], acc(0, 96))
            link(V.tensor_copy(fconvw[:, :, :], acc(1, 132).rearrange("p (i c) -> p i c", i=3)))
            dve.nop().then_inc(sem("taps_done"), 1)
            upto(dve, "rel_in", 16)
            V.tensor_copy(stage_bt[:, 0:P], stage_rb[:, 0:1].broadcast_to([AH, P]))
            for k, lo, hi in bucket_ranges():
                if k == 0:
                    continue
                last = V.tensor_copy(stage_bt[:, P - 1 + lo:P - 1 + hi],
                                     stage_rb[:, k:k + 1].broadcast_to([AH, hi - lo]))
            last = V.tensor_copy(stage_bt[:, P - 1 + S:3 * P], stage_rb[:, 0:1].broadcast_to([AH, 1]))
            last.then_inc(sem("rel_built"), 1)
            upto(dve, "const_done", 1)
            upto(dve, "rowc_in", 16 * 8)
            link(V.tensor_copy(posf, posi[:, :]))
            C1 = 6.28125
            C2 = float(np.float32(2 * np.pi - C1))
            C2 = float(np.frombuffer((np.frombuffer(np.float32(C2).tobytes(), np.uint32) & np.uint32(0xfffff000)).tobytes(), np.float32)[0])
            C3 = float(np.float32(2 * np.pi - C1 - C2))
            csv = cs.rearrange("p (c t i) -> p c t i", c=2, t=NT)
            tmpn = gx[:, :, 0:16]
            for t in range(NT):
                last = V.tensor_scalar(csv[:, 0, t, :], rc_freq, posf[:, t:t + 1], None, ALU.mult)
            link(last)
            link(V.tensor_scalar(tmpn, csv[:, 0], float(1 / (2 * np.pi)), 12582912.0, ALU.mult, ALU.add))
            link(V.tensor_scalar(tmpn, tmpn, 12582912.0, None, ALU.subtract))
            for C in (C1, C2, C3):
                link(V.scalar_tensor_tensor(csv[:, 0], tmpn, -C, csv[:, 0], ALU.mult, ALU.add))
            PI = 3.1415925
            link(V.tensor_scalar(csv[:, 0], csv[:, 0], PI, -PI, ALU.min, ALU.max))
            link(V.scalar_tensor_tensor(csv[:, 1], csv[:, 0], -1.0, csv[:, 0], ALU.mult, ALU.max))
            V.tensor_scalar(csv[:, 1], csv[:, 1], -1.0, float(np.pi / 2), ALU.mult, ALU.add)\
             .then_inc(sem("angle_done"), 1)
            for m in range(1, 6):
                ahead(fm_blocks[m] + 1)
                if m == 2:
                    upto(dve, "gt_done", 2)
                    link(V.tensor_copy(gains[:, KD:n_gain_rows], acc(0, n_gain_rows - KD)))
                    V.memset(gains[64:P, g_c3:g_c3 + 2], 1.0)\
                     .then_inc(sem("gains_done"), 1)
                conv4(m - 1)
            ahead(blk_small + 1)
            conv4(5)
            delta_rule_dve(dve, V, link, ahead)
            upto(dve, "ro_done", 1)
            upto(dve, "gz_done", 1)
            for u in range(16):
                v = unit(DA)[:, u, :]
                last = V.scalar_tensor_tensor(v, v, oss[:, u:u + 1], GATE[:, u, :], ALU.mult, ALU.mult)
            last.then_inc(t_ready, 1)
            for m in range(6, 10):
                ahead(fm_blocks[m] + 1)
                if m >= 7:
                    fox_scale(dve, V, m - 1)
            ahead(blk_fv[0] + 1)
            fox_scale(dve, V, 9)
            ahead(blk_fv[1] + 1)
            core(0)
            for it in blk_gf + blk_gg:
                ahead(it + 1)
            for n, (st, blocks, gate) in enumerate(((t_gdn, blk_bg, 1), (t_fox, blk_bf, 0))):
                transpose_stage(st)
                for j, it in enumerate(blocks):
                    ahead(it + 1)
                    g = gid(it)
                    evacuated(dve, (blk_gg if gate == 1 else blk_gf)[j])
                    accumulated(dve, it)
                    for t in range(NT):
                        cols = slice(j * COLS, (j + 1) * COLS)
                        dst = tok(Y_SUM)[:, t, cols] if n == 0 else tok(gate)[:, t, cols]
                        last = V.tensor_tensor(dst, tok(gate)[:, t, cols], bank(g, t), ALU.mult)
                    last.then_inc(blk_free(g), 1)
                    if n == 1:
                        evacuated(dve, it)
                        V.tensor_tensor(tok(Y_SUM)[:, :, cols], tok(Y_SUM)[:, :, cols], tok(gate)[:, :, cols],
                                        ALU.add).then_inc(t_ready, 1)
            transpose_stage(t_y)
            upto(dve, "x_again", 16)
            residual_blocks(blk_wo)
            transpose_stage(t_ffn[0])
            ffn(0, it_ffn[0])
            ahead(it_ffn[0] + 1)
            accumulated(dve, it_ffn[0])
            add_to_x(sem("xf_done"))
            dve.wait_ge(r_done, 3)
            upto(dve, "nf_in", 16)
            for half in range(2):
                cols = slice(half * COLS, (half + 1) * COLS)
                for t in range(NT):
                    last = V.scalar_tensor_tensor(X[:, t, cols], X[:, t, cols], r_tok[:, t:t + 1],
                                                  slot(2, D)[:, cols], ALU.mult, ALU.mult)
                last.then_inc(t_ready, 1)

            for layer in range(layers):
                b, kind = layer_blocks[layer], layer % 3
                transpose_stage(t_mix[layer])
                if kind == 2:
                    latent_dve(dve, V, link, b, ahead)
                else:
                    short_dve(dve, V, link, b, ahead, layer)
                core(layer + 1)
                transpose_stage(t_att[layer])
                residual_blocks(b["out"])
                transpose_stage(t_ffn[layer + 1])
                ffn(layer + 1, it_ffn[layer + 1])
                ahead(it_ffn[layer + 1] + 1)
                accumulated(dve, it_ffn[layer + 1])
                add_to_x(t_ready)

        @block.tensor
        def _(pe):
            M = pe.matmul
            second_half = [None]

            def use(c, it, outs, lh, ll, k0, first, last):
                pe.wait_ge(split_done, c + 1 if it is None else it * 8 + (c + 1 - 8))
                ch = chunks[c]
                w_hi = wh[:, c % SPL, 0:size(c)].rearrange("p (k n) -> p k n", k=ch.nk)
                w_lo = wl[:, c % SPL, 0:size(c)].rearrange("p (k n) -> p k n", k=ch.nk)
                for k in range(ch.nk):
                    if second_half[0] and lh is hTh and k0 + k == KD // 2:
                        pe.wait_ge(t_split, second_half[0])
                        second_half[0] = None
                    for t in range(NT):
                        a_hi = lh[:, k0 + k, t * P:(t + 1) * P]
                        a_lo = ll[:, k0 + k, t * P:(t + 1) * P]
                        M(outs[t], a_hi, w_hi[:, k, :], start=first and k == 0, stop=False)
                        M(outs[t], a_hi, w_lo[:, k, :], start=False, stop=False)
                        ins = M(outs[t], a_lo, w_hi[:, k, :], start=False, stop=last and k == ch.nk - 1)
                ins.then_inc(spl_free, 1)

            def block_mm(it, lh=hTh, ll=hTl, k_first=0):
                _, c0, cs_, g = items[it]
                if g >= 2:
                    pe.wait_ge(blk_free(g), g // 2)
                k0 = k_first
                w = cs_[0].w
                for i, ch in enumerate(cs_):
                    use(c0 + i, None, [bank(g, t, w) for t in range(NT)], lh, ll, k0, i == 0, i == len(cs_) - 1)
                    k0 += ch.nk

            def transposes(pairs, signal):
                for dst, src in pairs:
                    k = src.shape[0]
                    last = pe.transpose(dst, src, ident[0:k, 0:k])
                last.then_inc(signal, 1)

            def transpose_stage(n):
                src = T_STAGES[n][0]
                for half in range(2):
                    ready(pe, n, half)
                    dst = TP if half == 0 else AC
                    off = 0 if half == 0 else 2 * COLS
                    transposes([(dst[:, off + k * S + t * P:off + k * S + (t + 1) * P],
                                 src[:, t, (4 * half + k) * P:(4 * half + k + 1) * P])
                                for k in range(4) for t in range(NT)], t_done)

            def hidden(n):
                pe.wait_ge(t_split, 2 * n + 1)
                second_half[0] = 2 * n + 2

            def core(n):
                c = core_list[n]
                h0 = core_base[n]
                dv = c["dv"]
                for i in range(c["heads"] + 2):
                    if i < c["heads"]:
                        if i >= 2:
                            pe.wait_ge(lg_done, h0 + i - 1)
                        dst = acc(2 + i % 2, 3 * P)
                        if n == 0:
                            upto(pe, "lf_done", i + 1)
                            own = lf[:, 1, i:i + 1].broadcast_to([P, P])
                            gates = {(0, 0): ((tri, LF(i, 0)),),
                                     (1, 0): ((ones, LF(i, 0)), (tri, own)),
                                     (1, 1): ((tri, LF(i, 1)),)}
                            for (t, kt), terms in gates.items():
                                part = dst[:, (t + kt) * P:(t + kt + 1) * P]
                                M(part, c["q"](i, t), c["k"](i)[:, kt * P:(kt + 1) * P], start=True, stop=False)
                                for m, (lhs, rhs) in enumerate(terms):
                                    last = M(part, lhs[:, :], rhs, start=False, stop=m == len(terms) - 1)
                        else:
                            M(dst[:, 0:P], c["q"](i, 0), c["k"](i)[:, 0:P], start=True, stop=True)
                            last = M(dst[:, P:3 * P], c["q"](i, 1), c["k"](i), start=True, stop=True)
                        last.then_inc(s_done, 1)
                    if 1 <= i <= c["heads"]:
                        h = i - 1
                        pe.wait_ge(p_done, h0 + h + 1)
                        if h >= 2:
                            pe.wait_ge(pe_done, h0 + h - 1)
                        transposes([(tpb(h % 2, P, s * P), LG[:, h % 2, s * P:(s + 1) * P]) for s in range(3)], pt_done)
                    if i >= 2:
                        h = i - 2
                        pe.wait_ge(pe_done, h0 + h + 1)
                        if h >= 2:
                            pe.wait_ge(o_done, h0 + h - 1)
                        b = h % 2
                        M(acc(b, dv), PTs[:, b, 0:P], c["v"](h, 0), start=True, stop=True)
                        M(acc(b, dv, P), PTs[:, b, P:2 * P], c["v"](h, 0), start=True, stop=False)
                        M(acc(b, dv, P), PTs[:, b, 2 * P:3 * P], c["v"](h, 1), start=False, stop=True)\
                            .then_inc(pv_done, 1)
                if n == 0:
                    pe.wait_ge(o_done, h0 + c["heads"])

            def ffn(f, it):
                n, b = it_n[f], it_base[f]
                c0 = items[it][1]
                ups = [up(t) for t in range(NT)]

                def up_mm(c, j):
                    for k in range(4):
                        use(c + k, j, ups, hTh, hTl, 2 * k, k == 0, k == 3)

                def dn_mm(c, j, first, last):
                    for k in range(4):
                        cb = k % 2
                        use(c + k, j, [acc(2 * t + cb) for t in range(NT)], uTh, uTl,
                            (2 if f > 0 else 1) * (k // 2), first and k < 2, last and k >= 2)

                def transpose_hidden(j):
                    if f > 0:
                        pe.wait_ge(sq_done, j + (b - it_base[1] + 1))
                        cols = lambda t, k: hid[:, t * COLS + k * P:t * COLS + (k + 1) * P]
                    else:
                        pe.wait_ge(hid_done, j + (b + 1))
                        cols = lambda t, k: hid[:, t * COLS + k * P:t * COLS + (k + 1) * P]
                    transposes([(TP[:, k * S + t * P:k * S + (t + 1) * P], cols(t, k))
                                for k in range(4) for t in range(NT)], ut_done)

                up_mm(c0, None)
                transpose_hidden(0)
                up_mm(c0 + 4, None)
                pe.wait_ge(ul_done, b + 1)
                dn_mm(c0 + 8, None, True, False)
                transpose_hidden(1)
                with pe.Fori(2, n) as j:
                    up_mm(c0 + 4, j)
                    pe.wait_ge(ul_done, j + b)
                    dn_mm(c0 + 8, j, False, False)
                    transpose_hidden(j)
                pe.wait_ge(ul_done, b + n)
                dn_mm(c0 + 4 + 8 * (n - 1), None, False, True)

            upto(pe, "ident_done", 1)
            transpose_stage(t_in1)
            upto(pe, "mix_in", 16)
            transposes([(up(0, KD), stage0[0:KD, :])], sem("gt_done"))
            hidden(t_in1)

            def feature_transpose(m):
                evacuated(pe, fm_blocks[m])
                if m >= 1:
                    pe.wait_ge(fm_done, m)
                transposes([(TP[:, k * S + t * P:k * S + (t + 1) * P], tk(m)[:, t, k * P:(k + 1) * P])
                            for k in range(4) for t in range(NT)], ft_done)

            upto(pe, "gains_done", 1)
            for m in range(6):
                block_mm(fm_blocks[m])
                if m == 0:
                    upto(pe, "taps_in", 16 * 4)
                    transposes([(acc(0, 96), stage2[0:96, :])] +
                               [(acc(1, 44, 44 * i), stage3[0:44, i, :]) for i in range(3)], sem("taps_ps"))
                    upto(pe, "taps_done", 1)
                if m == 2:
                    upto(pe, "rows_in", 16 * sum(2 if half else 1 for _, _, half in row_src[1:]))
                    evacuated(pe, fm_blocks[1])
                    transposes([(acc(0, n_gain_rows - KD), stage1[0:n_gain_rows - KD, :])], sem("gt_done"))
                    upto(pe, "gains_done", 2)
                if m >= 1:
                    feature_transpose(m - 1)
            block_mm(blk_small)
            feature_transpose(5)
            for it in blk_gz:
                block_mm(it)
            delta_rule_pe(pe, M, transposes)
            upto(pe, "o1_done", 2)
            for m in range(6, 10):
                block_mm(fm_blocks[m])
                if m >= 7:
                    feature_transpose(m - 1)
            block_mm(blk_fv[0])
            feature_transpose(9)
            block_mm(blk_fv[1])
            evacuated(pe, blk_fv[0])
            evacuated(pe, blk_fv[1])
            pe.wait_ge(fm_done, 10)
            core(0)
            for it in blk_gf + blk_gg:
                block_mm(it)
            for st, blocks in ((t_gdn, blk_bg), (t_fox, blk_bf), (t_y, blk_wo)):
                transpose_stage(st)
                hidden(st)
                for it in blocks:
                    block_mm(it)
            transpose_stage(t_ffn[0])
            hidden(t_ffn[0])
            ffn(0, it_ffn[0])
            for layer in range(layers):
                b, kind = layer_blocks[layer], layer % 3
                transpose_stage(t_mix[layer])
                hidden(t_mix[layer])
                if kind == 2:
                    latent_pe(pe, M, transposes, b, block_mm)
                else:
                    short_pe(pe, M, transposes, b, block_mm, layer)
                core(layer + 1)
                transpose_stage(t_att[layer])
                hidden(t_att[layer])
                for it in b["out"]:
                    block_mm(it)
                transpose_stage(t_ffn[layer + 1])
                hidden(t_ffn[layer + 1])
                ffn(layer + 1, it_ffn[layer + 1])


_INS = ["x", "norm_mix", "w_in", "fox_f_bias", "gdn_conv_w", "gdn_a_log", "gdn_dt_bias", "gdn_norm",
        "w_branch_fox", "w_branch_gdn", "w_out", "norm_ffn", "w_up", "ffn_conv_w", "w_down", "norm_final",
        "positions_2", "rel_bias_2", "norm_mix_2", "norm_mlp_2", "w_up_2", "w_down_2",
        "a_w_in_2", "a_q_gain_2", "a_k_gain_2", "a_w_out_2",
        "b_w_in_2", "b_q_gain_2", "b_k_gain_2", "b_sinks_2", "b_w_out_2",
        "c_w_in_2", "c_q_a_gain_2", "c_w_q_b_2", "c_kv_a_gain_2", "c_w_kv_b_2", "c_q_gain_2", "c_k_gain_2",
        "c_w_out_2"]


def kernel(**inputs):
    import concourse.bacc as bacc
    from concourse.bass_utils import run_bass_kernel_spmd

    nc = bacc.Bacc("TRN2", target_bir_lowering=False, num_devices=1)
    arrays, args = {}, {}
    for name in _INS:
        a = np.ascontiguousarray(inputs[name])
        arrays[f"in_{name}"] = a
        args[name] = nc.dram_tensor(f"in_{name}", a.shape, mybir.dt.from_np(a.dtype), kind="ExternalInput").ap()
    args["out"] = nc.dram_tensor("out_0", (1, S, D), F32, kind="ExternalOutput").ap()
    build(nc, **args)
    r = run_bass_kernel_spmd(nc, [arrays], core_ids=[0])
    return r.results[0]["out_0"]
```
